# Optimizing a Trainium2 kernel written in Bass

```python
import math
import jax, jax.numpy as jnp
from jax import lax
import numpy as np

D_MODEL = 1024
BATCH = 1
SEQ = 1024
DEPTH = 1

N_MIXERS = 2
N_SB_LAYERS = (DEPTH + N_MIXERS - 1) // N_MIXERS
N_NSA_LAYERS = DEPTH // N_MIXERS
N_HEADS = 16
HEAD_DIM = 64
MIX_WIDTH = N_HEADS * HEAD_DIM
N_KV_HEADS = 4
GROUP = N_HEADS // N_KV_HEADS
SB_IN = 3 * MIX_WIDTH
NSA_IN = MIX_WIDTH + 6 * N_KV_HEADS * HEAD_DIM + 3 * N_HEADS
D_FF = ((8 * D_MODEL + 2) // 3 + 255) // 256 * 256
PLE_DIM = 256
Q_BLOCK = 128
REL_BUCKETS = 32
REL_MAX_DIST = 128
CMP_LEN = 32
CMP_STRIDE = 16
CMP_HIDDEN = 256
SEL_LEN = 64
SEL_TOPK = 16
WINDOW = 512
FORCED_SCORE = 100.0
EPS = 1e-6


def rms_norm(x, g):
    xf = x.astype(jnp.float32)
    y = xf * lax.rsqrt(jnp.mean(xf * xf, axis=-1, keepdims=True) + EPS)
    return (y * g.astype(jnp.float32)).astype(x.dtype)

def rel_bucket(dist):
    n = jnp.maximum(dist, 0)
    exact = REL_BUCKETS // 2
    nf = jnp.maximum(n, 1).astype(jnp.float32)
    large = exact + (jnp.log(nf / exact) / math.log(REL_MAX_DIST / exact)
                     * (REL_BUCKETS - exact)).astype(jnp.int32)
    large = jnp.minimum(large, REL_BUCKETS - 1)
    return jnp.where(n < exact, n, large)

def swiglu(x, w_in, w_out):
    a, b = jnp.split(x @ w_in, 2, axis=-1)
    return (jax.nn.silu(a) * b) @ w_out

def stick_breaking_attention(h, w_in, w_out):
    B, S, _ = h.shape
    qkv = (h @ w_in).reshape(B, S, 3, N_HEADS, HEAD_DIM).transpose(2, 0, 3, 1, 4)
    q, k, v = qkv[0], qkv[1], qkv[2]
    scale = HEAD_DIM ** -0.5
    kpos = jnp.arange(S)

    def block(q0):
        qb = lax.dynamic_slice_in_dim(q, q0, Q_BLOCK, axis=2)
        z = jnp.einsum('bhqd,bhkd->bhqk', qb, k).astype(jnp.float32) * scale
        t = q0 + jnp.arange(Q_BLOCK)
        causal = kpos[None, :] < t[:, None]
        log_fail = jnp.where(causal, jax.nn.log_sigmoid(-z), 0.0)
        after = lax.cumsum(log_fail, axis=3, reverse=True) - log_fail
        a = jnp.where(causal, jnp.exp(jax.nn.log_sigmoid(z) + after), 0.0)
        return jnp.einsum('bhqk,bhkd->bhqd', a, v.astype(jnp.float32))

    out = lax.map(block, jnp.arange(0, S, Q_BLOCK))
    out = out.transpose(1, 0, 3, 2, 4).reshape(B, S, MIX_WIDTH).astype(h.dtype)
    return out @ w_out

def native_sparse_attention(h, w_in, w_out, rel_bias, pe_k, pe_v,
                            ck_w1, ck_w2, cv_w1, cv_w2):
    B, S, _ = h.shape
    scale = HEAD_DIM ** -0.5
    proj = h @ w_in
    q = proj[..., :MIX_WIDTH].reshape(B, S, N_KV_HEADS, GROUP, HEAD_DIM)
    q = q.transpose(0, 2, 3, 1, 4)
    kv_end = MIX_WIDTH + 6 * N_KV_HEADS * HEAD_DIM
    kv = proj[..., MIX_WIDTH:kv_end].reshape(B, S, 6, N_KV_HEADS, HEAD_DIM)
    kv = kv.transpose(2, 0, 3, 1, 4)
    k_cmp, v_cmp, k_sel, v_sel, k_win, v_win = (kv[i] for i in range(6))
    gates = jax.nn.sigmoid(proj[..., kv_end:].astype(jnp.float32))
    gates = gates.reshape(B, S, 3, N_KV_HEADS, GROUP).transpose(2, 0, 3, 4, 1)

    n_cmp = (S - CMP_LEN) // CMP_STRIDE + 1
    win_idx = jnp.arange(n_cmp)[:, None] * CMP_STRIDE + jnp.arange(CMP_LEN)[None, :]

    def compress(kx, pe, w1, w2):
        blocks = kx[:, :, win_idx] + pe
        flat = blocks.reshape(B, N_KV_HEADS, n_cmp, CMP_LEN * HEAD_DIM)
        return jax.nn.gelu(flat @ w1) @ w2

    kc = compress(k_cmp, pe_k, ck_w1, ck_w2)
    vc = compress(v_cmp, pe_v, cv_w1, cv_w2)
    cmp_start = jnp.arange(n_cmp) * CMP_STRIDE
    cmp_end = cmp_start + CMP_LEN - 1

    n_sel = S // SEL_LEN
    top_k = min(SEL_TOPK, n_sel)
    sel_ids = jnp.arange(n_sel)
    sel_start = sel_ids * SEL_LEN
    overlap = ((cmp_start[:, None] < sel_start[None, :] + SEL_LEN)
               & (cmp_start[:, None] + CMP_LEN > sel_start[None, :])).astype(jnp.float32)
    ks_b = k_sel.reshape(B, N_KV_HEADS, n_sel, SEL_LEN, HEAD_DIM)
    vs_b = v_sel.reshape(B, N_KV_HEADS, n_sel, SEL_LEN, HEAD_DIM)
    b_i = jnp.arange(B)[:, None, None, None]
    h_i = jnp.arange(N_KV_HEADS)[None, :, None, None]
    h_i5 = h_i[..., None]
    table_t = rel_bias.reshape(REL_BUCKETS, N_KV_HEADS, GROUP).transpose(1, 0, 2)

    pad = ((0, 0), (0, 0), (WINDOW, 0), (0, 0))
    kw_pad = jnp.pad(k_win, pad)
    vw_pad = jnp.pad(v_win, pad)
    slab = Q_BLOCK + WINDOW
    dist_w = jnp.arange(Q_BLOCK)[:, None] - jnp.arange(slab)[None, :] + WINDOW
    band = (dist_w >= 0) & (dist_w < WINDOW)
    bias_w = rel_bias[rel_bucket(dist_w)].reshape(Q_BLOCK, slab, N_KV_HEADS, GROUP)
    bias_w = bias_w.transpose(2, 3, 0, 1).astype(jnp.float32)

    def block(q0):
        t = q0 + jnp.arange(Q_BLOCK)
        qb = lax.dynamic_slice_in_dim(q, q0, Q_BLOCK, axis=3)

        dist_c = t[:, None] - cmp_end[None, :]
        bias_c = rel_bias[rel_bucket(dist_c)].reshape(Q_BLOCK, n_cmp, N_KV_HEADS, GROUP)
        bias_c = bias_c.transpose(2, 3, 0, 1).astype(jnp.float32)
        s_c = jnp.einsum('bhgqd,bhnd->bhgqn', qb, kc).astype(jnp.float32) * scale + bias_c
        s_c = jnp.where(dist_c >= 0, s_c, -jnp.inf)
        m_c = jnp.max(s_c, axis=-1, keepdims=True)
        e_c = jnp.exp(s_c - jnp.where(jnp.isfinite(m_c), m_c, 0.0))
        den_c = jnp.sum(e_c, axis=-1, keepdims=True)
        p_c = e_c / jnp.where(den_c > 0, den_c, 1.0)
        o_c = jnp.einsum('bhgqn,bhnd->bhgqd', p_c, vc.astype(jnp.float32))

        imp = jnp.einsum('bhgqn,ns->bhqs', p_c, overlap)
        cur = t // SEL_LEN
        forced = ((sel_ids[None, :] == 0) | (sel_ids[None, :] == cur[:, None])
                  | (sel_ids[None, :] == cur[:, None] - 1))
        causal_blk = sel_ids[None, :] <= cur[:, None]
        imp = jnp.where(forced, FORCED_SCORE, jnp.where(causal_blk, imp, -1.0))
        _, idx = lax.top_k(imp, top_k)
        kg = ks_b[b_i, h_i, idx]
        vg = vs_b[b_i, h_i, idx]
        pos = idx[..., None] * SEL_LEN + jnp.arange(SEL_LEN)
        dist_s = t[None, None, :, None, None] - pos
        bias_s = jnp.moveaxis(table_t[h_i5, rel_bucket(dist_s)], -1, 2).astype(jnp.float32)
        s_s = jnp.einsum('bhgqd,bhqkld->bhgqkl', qb, kg).astype(jnp.float32) * scale + bias_s
        s_s = jnp.where((dist_s >= 0)[:, :, None], s_s, -jnp.inf)
        s_s = s_s.reshape(B, N_KV_HEADS, GROUP, Q_BLOCK, top_k * SEL_LEN)
        p_s = jax.nn.softmax(s_s, axis=-1).reshape(B, N_KV_HEADS, GROUP, Q_BLOCK, top_k, SEL_LEN)
        o_s = jnp.einsum('bhgqkl,bhqkld->bhgqd', p_s, vg.astype(jnp.float32))

        kw = lax.dynamic_slice_in_dim(kw_pad, q0, slab, axis=2)
        vw = lax.dynamic_slice_in_dim(vw_pad, q0, slab, axis=2)
        ok_w = band & ((q0 - WINDOW + jnp.arange(slab)) >= 0)[None, :]
        s_w = jnp.einsum('bhgqd,bhkd->bhgqk', qb, kw).astype(jnp.float32) * scale + bias_w
        p_w = jax.nn.softmax(jnp.where(ok_w, s_w, -jnp.inf), axis=-1)
        o_w = jnp.einsum('bhgqk,bhkd->bhgqd', p_w, vw.astype(jnp.float32))

        g = lax.dynamic_slice_in_dim(gates, q0, Q_BLOCK, axis=4)[..., None]
        return g[0] * o_c + g[1] * o_s + g[2] * o_w

    out = lax.map(block, jnp.arange(0, S, Q_BLOCK))
    out = out.transpose(1, 0, 4, 2, 3, 5).reshape(B, S, MIX_WIDTH).astype(h.dtype)
    return out @ w_out

def first_inputs(seed: int = 0) -> dict:
    key = jax.random.key(seed)
    ks = jax.random.split(key, 24)
    f32 = jnp.float32

    def nrm(k, shape, scale):
        return jax.random.normal(k, shape, f32) * scale

    def gain(k, shape):
        return 1.0 + 0.01 * jax.random.normal(k, shape, f32)

    return {
        "x": nrm(ks[0], (BATCH, SEQ, D_MODEL), 1.0),
        "p": nrm(ks[1], (DEPTH, BATCH, SEQ, PLE_DIM), 1.0),
        "rel_bias": nrm(ks[2], (REL_BUCKETS, N_HEADS), 0.5),
        "norm_mix": gain(ks[3], (DEPTH, D_MODEL)),
        "norm_ffn": gain(ks[4], (DEPTH, D_MODEL)),
        "norm_ple": gain(ks[5], (DEPTH, D_MODEL)),
        "final_norm": gain(ks[6], (D_MODEL,)),
        "sb_w_in": nrm(ks[7], (N_SB_LAYERS, D_MODEL, SB_IN), D_MODEL ** -0.5),
        "sb_w_out": nrm(ks[8], (N_SB_LAYERS, MIX_WIDTH, D_MODEL), MIX_WIDTH ** -0.5),
        "nsa_w_in": nrm(ks[9], (N_NSA_LAYERS, D_MODEL, NSA_IN), D_MODEL ** -0.5),
        "nsa_w_out": nrm(ks[10], (N_NSA_LAYERS, MIX_WIDTH, D_MODEL), MIX_WIDTH ** -0.5),
        "nsa_pe_k": nrm(ks[11], (N_NSA_LAYERS, CMP_LEN, HEAD_DIM), 0.02),
        "nsa_pe_v": nrm(ks[12], (N_NSA_LAYERS, CMP_LEN, HEAD_DIM), 0.02),
        "nsa_ck_w1": nrm(ks[13], (N_NSA_LAYERS, CMP_LEN * HEAD_DIM, CMP_HIDDEN), (CMP_LEN * HEAD_DIM) ** -0.5),
        "nsa_ck_w2": nrm(ks[14], (N_NSA_LAYERS, CMP_HIDDEN, HEAD_DIM), CMP_HIDDEN ** -0.5),
        "nsa_cv_w1": nrm(ks[15], (N_NSA_LAYERS, CMP_LEN * HEAD_DIM, CMP_HIDDEN), (CMP_LEN * HEAD_DIM) ** -0.5),
        "nsa_cv_w2": nrm(ks[16], (N_NSA_LAYERS, CMP_HIDDEN, HEAD_DIM), CMP_HIDDEN ** -0.5),
        "ffn_w_in": nrm(ks[17], (DEPTH, D_MODEL, 2 * D_FF), D_MODEL ** -0.5),
        "ffn_w_out": nrm(ks[18], (DEPTH, D_FF, D_MODEL), D_FF ** -0.5),
        "ple_w_proj": nrm(ks[19], (DEPTH, PLE_DIM, D_MODEL), PLE_DIM ** -0.5),
        "ple_w_gate": nrm(ks[20], (DEPTH, D_MODEL, D_MODEL), D_MODEL ** -0.5),
    }

def first_block(x, p, rel_bias, norm_mix, norm_ffn, norm_ple, final_norm,
              sb_w_in, sb_w_out, nsa_w_in, nsa_w_out, nsa_pe_k, nsa_pe_v,
              nsa_ck_w1, nsa_ck_w2, nsa_cv_w1, nsa_cv_w2,
              ffn_w_in, ffn_w_out, ple_w_proj, ple_w_gate):
    h = x
    for i in range(DEPTH):
        j = i // N_MIXERS
        hn = rms_norm(h, norm_mix[i])
        if i % N_MIXERS == 0:
            mix = stick_breaking_attention(hn, sb_w_in[j], sb_w_out[j])
        else:
            mix = native_sparse_attention(hn, nsa_w_in[j], nsa_w_out[j], rel_bias,
                                          nsa_pe_k[j], nsa_pe_v[j], nsa_ck_w1[j],
                                          nsa_ck_w2[j], nsa_cv_w1[j], nsa_cv_w2[j])
        h = h + mix
        h = h + swiglu(rms_norm(h, norm_ffn[i]), ffn_w_in[i], ffn_w_out[i])
        gate = jax.nn.sigmoid(rms_norm(h, norm_ple[i]) @ ple_w_gate[i])
        h = h + gate * (p[i] @ ple_w_proj[i])
    return rms_norm(h, final_norm)


_first_inputs = first_inputs


def first_inputs(seed=0):
    import zlib

    import numpy as np

    out = dict(_first_inputs(seed))
    spreads = {}
    factors = {}
    for name, (base, spread) in spreads.items():
        noise = np.random.default_rng([zlib.crc32(name.encode()), seed]).standard_normal(out[name].shape)
        drawn = base * np.exp(spread * noise) if base else spread * noise
        out[name] = __import__('jax').numpy.asarray(drawn.astype(out[name].dtype))
    for name, factor in factors.items():
        out[name] = (out[name] * factor).astype(out[name].dtype)
    return out


_narrow_inputs = first_inputs


def first_inputs(seed=0):

    out = dict(_narrow_inputs(seed))
    wider = {'norm_mix': 10.08, 'norm_ffn': 10.66, 'norm_ple': 12.0, 'final_norm': 6.17}
    for name, times in wider.items():
        mean = out[name].mean()
        out[name] = (mean + times * (out[name] - mean)).astype(out[name].dtype)
    return out


EXPAND = 2
D_INNER = EXPAND * D_MODEL
D_CONV = D_INNER // 2
D_RET = D_INNER - D_CONV
RET_HEADS = 4
RET_QK_DIM = 256
RET_V_DIM = D_RET // RET_HEADS
CONV_WIDTH = 31
CHUNK = 128
ROPE_BASE = 10000.0
NORM_EPS = 1e-6
N_IN = 3 * D_CONV + 2 * RET_HEADS * RET_QK_DIM + 2 * D_RET


def _rmsnorm(x, g):
    x32 = x.astype(jnp.float32)
    y = x32 * lax.rsqrt(jnp.mean(x32 * x32, axis=-1, keepdims=True) + NORM_EPS)
    return (y * g.astype(jnp.float32)).astype(x.dtype)

def _layernorm(x, g, b):
    x32 = x.astype(jnp.float32)
    mu = jnp.mean(x32, axis=-1, keepdims=True)
    var = jnp.mean(jnp.square(x32 - mu), axis=-1, keepdims=True)
    y = (x32 - mu) * lax.rsqrt(var + NORM_EPS)
    return (y * g.astype(jnp.float32) + b.astype(jnp.float32)).astype(x.dtype)

def _rotary(x):
    s, dh = x.shape[1], x.shape[-1]
    inv_freq = 1.0 / (ROPE_BASE ** jnp.linspace(0.0, 1.0, dh // 2, dtype=jnp.float32))
    pos = jnp.arange(s, dtype=jnp.float32)
    theta = pos[:, None] * inv_freq[None, :]
    cos = jnp.cos(theta)[None, :, None, :]
    sin = jnp.sin(theta)[None, :, None, :]
    x32 = x.astype(jnp.float32)
    x1, x2 = x32[..., : dh // 2], x32[..., dh // 2:]
    out = jnp.concatenate([x1 * cos - x2 * sin, x1 * sin + x2 * cos], axis=-1)
    return out.astype(x.dtype)

def _causal_depthwise_conv(u, w, b):
    c = u.shape[-1]
    kern = w.astype(u.dtype)[:, None, :]
    y = lax.conv_general_dilated(
        u, kern, window_strides=(1,), padding=[(CONV_WIDTH - 1, 0)],
        dimension_numbers=("NWC", "WIO", "NWC"), feature_group_count=c)
    return y + b.astype(u.dtype)

def _retention_chunkwise(q, k, v):
    bsz, s, h, dk = q.shape
    dv = v.shape[-1]
    n = s // CHUNK

    def to_chunks(t):
        d = t.shape[-1]
        return t.astype(jnp.float32).reshape(bsz, n, CHUNK, h, d).transpose(1, 0, 3, 2, 4)

    qc, kc, vc = to_chunks(q), to_chunks(k), to_chunks(v)

    log_g = jnp.log(1.0 - jnp.exp2(-5.0 - jnp.arange(h, dtype=jnp.float32)))
    idx = jnp.arange(CHUNK, dtype=jnp.float32)
    diff = idx[:, None] - idx[None, :]
    decay_mask = jnp.where(diff >= 0,
                           jnp.exp(log_g[:, None, None] * jnp.maximum(diff, 0.0)[None]),
                           0.0)
    query_decay = jnp.exp(log_g[:, None] * (idx + 1.0)[None, :])
    key_decay = jnp.exp(log_g[:, None] * (CHUNK - 1.0 - idx)[None, :])
    chunk_decay = jnp.exp(log_g * CHUNK)

    def step(state, inp):
        q_i, k_i, v_i = inp
        scores = jnp.einsum("bhid,bhjd->bhij", q_i, k_i) * decay_mask[None]
        inner = jnp.einsum("bhij,bhjv->bhiv", scores, v_i)
        cross = jnp.einsum("bhid,bhdv->bhiv", q_i, state) * query_decay[None, :, :, None]
        new_state = state * chunk_decay[None, :, None, None] + jnp.einsum(
            "bhjd,bhjv->bhdv", k_i * key_decay[None, :, :, None], v_i)
        return new_state, inner + cross

    state0 = jnp.zeros((bsz, h, dk, dv), jnp.float32)
    _, out = lax.scan(step, state0, (qc, kc, vc))
    return out.transpose(1, 0, 3, 2, 4).reshape(bsz, s, h, dv)

def _head_groupnorm(o, g, b):
    mu = jnp.mean(o, axis=-1, keepdims=True)
    var = jnp.mean(jnp.square(o - mu), axis=-1, keepdims=True)
    y = ((o - mu) * lax.rsqrt(var + NORM_EPS)).reshape(o.shape[0], o.shape[1], -1)
    return y * g.astype(jnp.float32) + b.astype(jnp.float32)

def second_inputs(seed: int = 0) -> dict:
    key = jax.random.key(seed)
    ks = jax.random.split(key, 16)
    f32 = jnp.float32
    nrm = lambda k, shape, s: jax.random.normal(k, shape, f32) * s
    return {
        "x": nrm(ks[0], (BATCH, SEQ, D_MODEL), 1.0),
        "c": nrm(ks[1], (BATCH, D_MODEL), 1.0),
        "ada_w": nrm(ks[2], (DEPTH, D_MODEL, 3 * D_MODEL), 0.5 * D_MODEL ** -0.5),
        "ada_b": nrm(ks[3], (DEPTH, 3 * D_MODEL), 0.02),
        "norm_g": 1.0 + nrm(ks[4], (DEPTH, D_MODEL), 0.02),
        "w_in": nrm(ks[5], (DEPTH, D_MODEL, N_IN), D_MODEL ** -0.5),
        "conv_w": nrm(ks[6], (DEPTH, CONV_WIDTH, D_CONV), CONV_WIDTH ** -0.5),
        "conv_b": nrm(ks[7], (DEPTH, D_CONV), 0.02),
        "conv_ln_g": 1.0 + nrm(ks[8], (DEPTH, D_CONV), 0.02),
        "conv_ln_b": nrm(ks[9], (DEPTH, D_CONV), 0.02),
        "conv_pw": nrm(ks[10], (DEPTH, D_CONV, D_CONV), D_CONV ** -0.5),
        "ret_gn_g": 1.0 + nrm(ks[11], (DEPTH, D_RET), 0.02),
        "ret_gn_b": nrm(ks[12], (DEPTH, D_RET), 0.02),
        "w_out": nrm(ks[13], (DEPTH, D_INNER, D_MODEL), D_INNER ** -0.5),
        "final_g": 1.0 + nrm(ks[14], (D_MODEL,), 0.02),
    }

def second_block(x, c, ada_w, ada_b, norm_g, w_in, conv_w, conv_b, conv_ln_g, conv_ln_b,
              conv_pw, ret_gn_g, ret_gn_b, w_out, final_g):
    bsz, s, _ = x.shape
    dt = x.dtype
    c_act = jax.nn.silu(c)
    h = x
    for l in range(DEPTH):
        mod = c_act @ ada_w[l] + ada_b[l]
        shift, scale, gate = jnp.split(mod[:, None, :], 3, axis=-1)
        u = _rmsnorm(h, norm_g[l]) * (1.0 + scale) + shift

        proj = u @ w_in[l]
        o1 = D_CONV
        o2 = o1 + D_CONV
        o3 = o2 + D_CONV
        o4 = o3 + RET_HEADS * RET_QK_DIM
        o5 = o4 + RET_HEADS * RET_QK_DIM
        o6 = o5 + D_RET
        conv_a, conv_bp, conv_gate = proj[..., :o1], proj[..., o1:o2], proj[..., o2:o3]
        q = proj[..., o3:o4].reshape(bsz, s, RET_HEADS, RET_QK_DIM)
        k = proj[..., o4:o5].reshape(bsz, s, RET_HEADS, RET_QK_DIM)
        v = proj[..., o5:o6].reshape(bsz, s, RET_HEADS, RET_V_DIM)
        ret_gate = proj[..., o6:]

        a = conv_a * jax.nn.sigmoid(conv_bp)
        a = _causal_depthwise_conv(a, conv_w[l], conv_b[l])
        a = jax.nn.silu(_layernorm(a, conv_ln_g[l], conv_ln_b[l]))
        a = a @ conv_pw[l]
        y_conv = a * jax.nn.silu(conv_gate)

        q = _rotary(q)
        k = _rotary(k) * (RET_QK_DIM ** -0.5)
        r = _retention_chunkwise(q, k, v)
        r = _head_groupnorm(r, ret_gn_g[l], ret_gn_b[l]).astype(dt)
        y_ret = r * jax.nn.silu(ret_gate)

        y = jnp.concatenate([y_conv, y_ret], axis=-1) @ w_out[l]
        h = h + gate * y
    return _rmsnorm(h, final_g)


_first_inputs_2 = second_inputs


def second_inputs(seed=0):
    import zlib

    import numpy as np

    out = dict(_first_inputs_2(seed))
    spreads = {}
    factors = {'ada_b': 3.791,
     'norm_g': 8.0,
     'conv_b': 27.429,
     'conv_ln_g': 41.248,
     'conv_ln_b': 39.522,
     'ret_gn_g': 27.845,
     'ret_gn_b': 27.975,
     'final_g': 8.34}
    for name, (base, spread) in spreads.items():
        noise = np.random.default_rng([zlib.crc32(name.encode()), seed]).standard_normal(out[name].shape)
        drawn = base * np.exp(spread * noise) if base else spread * noise
        out[name] = __import__('jax').numpy.asarray(drawn.astype(out[name].dtype))
    for name, factor in factors.items():
        out[name] = (out[name] * factor).astype(out[name].dtype)
    return out


_narrow_inputs_2 = second_inputs


def second_inputs(seed=0):

    out = dict(_narrow_inputs_2(seed))
    wider = {'conv_ln_g': 4.64, 'conv_ln_b': 4.65, 'ret_gn_g': 4.6, 'ret_gn_b': 4.6, 'final_g': 3.26}
    for name, times in wider.items():
        mean = out[name].mean()
        out[name] = (mean + times * (out[name] - mean)).astype(out[name].dtype)
    return out


CHUNK_3 = 64
D_S5 = D_MODEL
S5_GROUP_CH = 16
S5_GROUPS = D_S5 // S5_GROUP_CH
S5_STATE = 64
D_SSD = D_MODEL
SSD_HEAD_DIM = 64
SSD_HEADS = D_SSD // SSD_HEAD_DIM
SSD_GROUPS = 4
SSD_HEADS_PER_GROUP = SSD_HEADS // SSD_GROUPS
SSD_STATE = 128
CONV_WIDTH_3 = 4
SSD_CONV_DIM = D_SSD + 2 * SSD_GROUPS * SSD_STATE
NORM_GROUP = D_SSD // SSD_GROUPS
MIX_WIDTH_3 = D_S5 + D_SSD
D_IN_PROJ = 2 * D_S5 + D_SSD + SSD_CONV_DIM + SSD_HEADS
SPLITS = (D_S5, 2 * D_S5, 2 * D_S5 + D_SSD, 2 * D_S5 + D_SSD + SSD_CONV_DIM)


def rmsnorm(x, w):
    xf = x.astype(jnp.float32)
    y = xf * lax.rsqrt(jnp.mean(xf * xf, axis=-1, keepdims=True) + EPS)
    return (y * w.astype(jnp.float32)).astype(x.dtype)

def gated_group_rmsnorm(y, z, w):
    g = y.astype(jnp.float32) * jax.nn.silu(z.astype(jnp.float32))
    b, l, d = g.shape
    g = g.reshape(b, l, SSD_GROUPS, NORM_GROUP)
    g = g * lax.rsqrt(jnp.mean(g * g, axis=-1, keepdims=True) + EPS)
    return (g.reshape(b, l, d) * w.astype(jnp.float32)).astype(y.dtype)

def causal_depthwise_conv(x, w, bias):
    k_w = w.shape[0]
    L = x.shape[1]
    xp = jnp.pad(x, ((0, 0), (k_w - 1, 0), (0, 0)))
    return sum(xp[:, k:k + L] * w[k] for k in range(k_w)) + bias

def segsum(a):
    T = a.shape[-1]
    cs = jnp.cumsum(a, axis=-1)
    diff = cs[..., :, None] - cs[..., None, :]
    mask = jnp.tril(jnp.ones((T, T), dtype=bool))
    return jnp.where(mask, diff, -jnp.inf)

def s5_branch(u, A_re, A_im, log_dt, B_re, B_im, C_re, C_im, D, w_glu, b_glu):
    f32 = jnp.float32
    b, L, _ = u.shape
    n_chunks = L // CHUNK_3
    uf = u.astype(f32)
    u_c = uf.reshape(b, n_chunks, CHUNK_3, S5_GROUPS, S5_GROUP_CH).transpose(1, 0, 2, 3, 4)
    A = lax.complex(A_re.astype(f32), A_im.astype(f32))
    dt = jnp.exp(log_dt.astype(f32))[:, None]
    A_bar = jnp.exp(A * dt)
    Bc = lax.complex(B_re.astype(f32), B_im.astype(f32))
    B_bar = ((A_bar - 1.0) / A)[..., None] * Bc
    Cc = lax.complex(C_re.astype(f32), C_im.astype(f32))
    steps = jnp.arange(1, CHUNK_3 + 1, dtype=f32)[:, None, None]
    pows = jnp.exp(A[None] * dt[None] * steps)

    def combine(e1, e2):
        a1, b1 = e1
        a2, b2 = e2
        return a1 * a2, a2 * b1 + b2

    def step(h0, uc):
        bu = jnp.einsum('btgh,gnh->btgn', uc, B_bar)
        a = jnp.broadcast_to(A_bar, bu.shape)
        _, local = lax.associative_scan(combine, (a, bu), axis=1)
        states = local + pows * h0[:, None]
        y = jnp.einsum('btgn,ghn->btgh', states, Cc).real
        return states[:, -1], y

    h0 = jnp.zeros((b, S5_GROUPS, S5_STATE), jnp.complex64)
    _, ys = lax.scan(step, h0, u_c)
    y = ys.transpose(1, 0, 2, 3, 4).reshape(b, L, D_S5) + D.astype(f32) * uf
    y = jax.nn.gelu(y)
    y = y * jax.nn.sigmoid(y @ w_glu.astype(f32) + b_glu.astype(f32))
    return y.astype(u.dtype)

def ssd_chunked(xs, dt, A, Bm, Cm):
    b, L, H, P = xs.shape
    c = L // CHUNK_3
    Bh = jnp.repeat(Bm, SSD_HEADS_PER_GROUP, axis=2).reshape(b, c, CHUNK_3, H, SSD_STATE)
    Ch = jnp.repeat(Cm, SSD_HEADS_PER_GROUP, axis=2).reshape(b, c, CHUNK_3, H, SSD_STATE)
    xd = (xs * dt[..., None]).reshape(b, c, CHUNK_3, H, P)
    a = (dt * A).reshape(b, c, CHUNK_3, H).transpose(0, 3, 1, 2)
    a_cs = jnp.cumsum(a, axis=-1)
    L_intra = jnp.exp(segsum(a))
    scores = jnp.einsum('bclhn,bcshn->bhcls', Ch, Bh) * L_intra
    y_diag = jnp.einsum('bhcls,bcshp->bclhp', scores, xd)
    decay_states = jnp.exp(a_cs[..., -1:] - a_cs)
    states = jnp.einsum('bclhn,bhcl,bclhp->bchpn', Bh, decay_states, xd)
    states = jnp.concatenate([jnp.zeros_like(states[:, :1]), states], axis=1)
    chunk_a = jnp.pad(a_cs[..., -1], ((0, 0), (0, 0), (1, 0)))
    decay_chunk = jnp.exp(segsum(chunk_a))
    new_states = jnp.einsum('bhzc,bchpn->bzhpn', decay_chunk, states)
    prev_states = new_states[:, :-1]
    y_off = jnp.einsum('bclhn,bchpn,bhcl->bclhp', Ch, prev_states, jnp.exp(a_cs))
    return (y_diag + y_off).reshape(b, L, H, P)

def ssd_branch(xBC, dt_raw, z, conv_w, conv_b, dt_bias, A_log, Dh, norm_w):
    f32 = jnp.float32
    b, L, _ = xBC.shape
    xBC = jax.nn.silu(causal_depthwise_conv(xBC, conv_w, conv_b))
    xs = xBC[..., :D_SSD].astype(f32).reshape(b, L, SSD_HEADS, SSD_HEAD_DIM)
    Bm = xBC[..., D_SSD:D_SSD + SSD_GROUPS * SSD_STATE].astype(f32).reshape(b, L, SSD_GROUPS, SSD_STATE)
    Cm = xBC[..., D_SSD + SSD_GROUPS * SSD_STATE:].astype(f32).reshape(b, L, SSD_GROUPS, SSD_STATE)
    dt = jax.nn.softplus(dt_raw.astype(f32) + dt_bias.astype(f32))
    A = -jnp.exp(A_log.astype(f32))
    y = ssd_chunked(xs, dt, A, Bm, Cm) + Dh.astype(f32)[:, None] * xs
    y = y.reshape(b, L, D_SSD).astype(z.dtype)
    return gated_group_rmsnorm(y, z, norm_w)

def third_inputs(seed: int = 0) -> dict:
    key = jax.random.key(seed)
    ks = jax.random.split(key, 26)
    f32 = jnp.float32
    nrm = lambda k, s, sc: jax.random.normal(k, s, f32) * sc
    x = jax.random.normal(ks[0], (BATCH, SEQ, D_MODEL), f32)
    p = jax.random.normal(ks[1], (DEPTH, BATCH, SEQ, PLE_DIM), f32)
    norm_w = 1.0 + nrm(ks[2], (DEPTH, D_MODEL), 0.02)
    w_in = nrm(ks[3], (DEPTH, D_MODEL, D_IN_PROJ), D_MODEL ** -0.5)
    n_idx = jnp.arange(S5_STATE, dtype=f32)
    s5_A_re = -0.5 + nrm(ks[4], (DEPTH, S5_GROUPS, S5_STATE), 0.01)
    s5_A_im = math.pi * n_idx + nrm(ks[5], (DEPTH, S5_GROUPS, S5_STATE), 0.01)
    s5_log_dt = jax.random.uniform(ks[6], (DEPTH, S5_GROUPS), f32, math.log(1e-3), math.log(1e-1))
    s5_B_re = nrm(ks[7], (DEPTH, S5_GROUPS, S5_STATE, S5_GROUP_CH), (2 * S5_GROUP_CH) ** -0.5)
    s5_B_im = nrm(ks[8], (DEPTH, S5_GROUPS, S5_STATE, S5_GROUP_CH), (2 * S5_GROUP_CH) ** -0.5)
    s5_C_re = nrm(ks[9], (DEPTH, S5_GROUPS, S5_GROUP_CH, S5_STATE), (2 * S5_STATE) ** -0.5)
    s5_C_im = nrm(ks[10], (DEPTH, S5_GROUPS, S5_GROUP_CH, S5_STATE), (2 * S5_STATE) ** -0.5)
    s5_D = nrm(ks[11], (DEPTH, D_S5), 1.0)
    s5_w_glu = nrm(ks[12], (DEPTH, D_S5, D_S5), D_S5 ** -0.5)
    s5_b_glu = nrm(ks[13], (DEPTH, D_S5), 0.01)
    conv_w = nrm(ks[14], (DEPTH, CONV_WIDTH_3, SSD_CONV_DIM), CONV_WIDTH_3 ** -0.5)
    conv_b = nrm(ks[15], (DEPTH, SSD_CONV_DIM), 0.01)
    dt0 = jnp.exp(jax.random.uniform(ks[16], (DEPTH, SSD_HEADS), f32, math.log(1e-3), math.log(1e-1)))
    dt_bias = dt0 + jnp.log(-jnp.expm1(-dt0))
    A_log = jnp.log(jax.random.uniform(ks[17], (DEPTH, SSD_HEADS), f32, 1.0, 16.0))
    ssd_D = 1.0 + nrm(ks[18], (DEPTH, SSD_HEADS), 0.1)
    ssd_norm_w = 1.0 + nrm(ks[19], (DEPTH, D_SSD), 0.02)
    w_out = nrm(ks[20], (DEPTH, MIX_WIDTH_3, D_MODEL), MIX_WIDTH_3 ** -0.5)
    ple_norm_w = 1.0 + nrm(ks[21], (DEPTH, D_MODEL), 0.02)
    w_ple_gate = nrm(ks[22], (DEPTH, D_MODEL, D_MODEL), D_MODEL ** -0.5)
    w_ple_proj = nrm(ks[23], (DEPTH, PLE_DIM, D_MODEL), PLE_DIM ** -0.5)
    final_norm_w = 1.0 + nrm(ks[24], (D_MODEL,), 0.02)
    return {"x": x, "p": p, "norm_w": norm_w, "w_in": w_in,
            "s5_A_re": s5_A_re, "s5_A_im": s5_A_im, "s5_log_dt": s5_log_dt,
            "s5_B_re": s5_B_re, "s5_B_im": s5_B_im, "s5_C_re": s5_C_re, "s5_C_im": s5_C_im,
            "s5_D": s5_D, "s5_w_glu": s5_w_glu, "s5_b_glu": s5_b_glu,
            "conv_w": conv_w, "conv_b": conv_b, "dt_bias": dt_bias, "A_log": A_log,
            "ssd_D": ssd_D, "ssd_norm_w": ssd_norm_w, "w_out": w_out,
            "ple_norm_w": ple_norm_w, "w_ple_gate": w_ple_gate, "w_ple_proj": w_ple_proj,
            "final_norm_w": final_norm_w}

def third_block(x, p, norm_w, w_in, s5_A_re, s5_A_im, s5_log_dt, s5_B_re, s5_B_im,
              s5_C_re, s5_C_im, s5_D, s5_w_glu, s5_b_glu, conv_w, conv_b, dt_bias,
              A_log, ssd_D, ssd_norm_w, w_out, ple_norm_w, w_ple_gate, w_ple_proj,
              final_norm_w):
    h = x
    for i in range(DEPTH):
        hn = rmsnorm(h, norm_w[i])
        proj = hn @ w_in[i]
        u_s5, z_s5, z_ssd, xBC, dt_raw = jnp.split(proj, SPLITS, axis=-1)
        y_s5 = s5_branch(u_s5, s5_A_re[i], s5_A_im[i], s5_log_dt[i], s5_B_re[i], s5_B_im[i],
                         s5_C_re[i], s5_C_im[i], s5_D[i], s5_w_glu[i], s5_b_glu[i])
        y_s5 = y_s5 * jax.nn.silu(z_s5)
        y_ssd = ssd_branch(xBC, dt_raw, z_ssd, conv_w[i], conv_b[i], dt_bias[i], A_log[i],
                           ssd_D[i], ssd_norm_w[i])
        h = h + jnp.concatenate([y_s5, y_ssd], axis=-1) @ w_out[i]
        gate = jax.nn.sigmoid(rmsnorm(h, ple_norm_w[i]) @ w_ple_gate[i])
        h = h + (p[i] @ w_ple_proj[i]) * gate
    return rmsnorm(h, final_norm_w)


_first_inputs_3 = third_inputs


def third_inputs(seed=0):
    import zlib

    import numpy as np

    out = dict(_first_inputs_3(seed))
    spreads = {}
    factors = {'norm_w': 3.39,
     's5_A_re': 64.0,
     's5_A_im': 64.0,
     's5_log_dt': 64.0,
     's5_B_re': 64.0,
     's5_B_im': 64.0,
     's5_C_re': 64.0,
     's5_C_im': 64.0,
     's5_b_glu': 40.449,
     'conv_b': 7.175,
     'ssd_norm_w': 18.251,
     'ple_norm_w': 64.0,
     'final_norm_w': 8.118,
     'ssd_D': 8.0}
    for name, (base, spread) in spreads.items():
        noise = np.random.default_rng([zlib.crc32(name.encode()), seed]).standard_normal(out[name].shape)
        drawn = base * np.exp(spread * noise) if base else spread * noise
        out[name] = __import__('jax').numpy.asarray(drawn.astype(out[name].dtype))
    for name, factor in factors.items():
        out[name] = (out[name] * factor).astype(out[name].dtype)
    return out


_narrow_inputs_3 = third_inputs


def third_inputs(seed=0):

    out = dict(_narrow_inputs_3(seed))
    wider = {'s5_b_glu': 3.25,
     'ssd_D': 6.06,
     'ssd_norm_w': 3.28,
     'ple_norm_w': 12.0,
     'final_norm_w': 3.2}
    for name, times in wider.items():
        mean = out[name].mean()
        out[name] = (mean + times * (out[name] - mean)).astype(out[name].dtype)
    return out


def setup_inputs(seed=0):
    out = dict(first_inputs(seed))
    for name, value in second_inputs(seed + 1).items():
        if name != "x":
            out[name + "_2"] = value
    for name, value in third_inputs(seed + 2).items():
        if name != "x":
            out[name + "_3"] = value
    return out


def reference(
    x, p, rel_bias, norm_mix, norm_ffn, norm_ple, final_norm, sb_w_in, sb_w_out, nsa_w_in,
    nsa_w_out, nsa_pe_k, nsa_pe_v, nsa_ck_w1, nsa_ck_w2, nsa_cv_w1, nsa_cv_w2, ffn_w_in,
    ffn_w_out, ple_w_proj, ple_w_gate, c_2, ada_w_2, ada_b_2, norm_g_2, w_in_2, conv_w_2,
    conv_b_2, conv_ln_g_2, conv_ln_b_2, conv_pw_2, ret_gn_g_2, ret_gn_b_2, w_out_2, final_g_2,
    p_3, norm_w_3, w_in_3, s5_A_re_3, s5_A_im_3, s5_log_dt_3, s5_B_re_3, s5_B_im_3, s5_C_re_3,
    s5_C_im_3, s5_D_3, s5_w_glu_3, s5_b_glu_3, conv_w_3, conv_b_3, dt_bias_3, A_log_3, ssd_D_3,
    ssd_norm_w_3, w_out_3, ple_norm_w_3, w_ple_gate_3, w_ple_proj_3, final_norm_w_3,
):
    x = first_block(
        x, p, rel_bias, norm_mix, norm_ffn, norm_ple, final_norm, sb_w_in, sb_w_out, nsa_w_in,
        nsa_w_out, nsa_pe_k, nsa_pe_v, nsa_ck_w1, nsa_ck_w2, nsa_cv_w1, nsa_cv_w2, ffn_w_in,
        ffn_w_out, ple_w_proj, ple_w_gate,
    )
    x = second_block(
        x, c_2, ada_w_2, ada_b_2, norm_g_2, w_in_2, conv_w_2, conv_b_2, conv_ln_g_2,
        conv_ln_b_2, conv_pw_2, ret_gn_g_2, ret_gn_b_2, w_out_2, final_g_2,
    )
    return third_block(
        x, p_3, norm_w_3, w_in_3, s5_A_re_3, s5_A_im_3, s5_log_dt_3, s5_B_re_3, s5_B_im_3,
        s5_C_re_3, s5_C_im_3, s5_D_3, s5_w_glu_3, s5_b_glu_3, conv_w_3, conv_b_3, dt_bias_3,
        A_log_3, ssd_D_3, ssd_norm_w_3, w_out_3, ple_norm_w_3, w_ple_gate_3, w_ple_proj_3,
        final_norm_w_3,
    )


_drawn_inputs = setup_inputs


def setup_inputs(seed=0):
    import zlib

    import numpy as np

    out = dict(_drawn_inputs(seed))
    spreads = {}
    factors = {'conv_b_3': 2.71, 'ple_norm_w_3': 4.004}
    for name, (base, spread) in spreads.items():
        noise = np.random.default_rng([zlib.crc32(name.encode()), seed]).standard_normal(out[name].shape)
        drawn = base * np.exp(spread * noise) if base else spread * noise
        out[name] = __import__('jax').numpy.asarray(drawn.astype(out[name].dtype))
    for name, factor in factors.items():
        out[name] = (out[name] * factor).astype(out[name].dtype)
    return out
```

```python
from contextlib import ExitStack

import numpy as np
import concourse.bass as bass
from concourse import mybir

P = 128
D = 1024
KT = D // P
T = 1024
HALF = T // 2
F32 = mybir.dt.float32
F32R = mybir.dt.float32r
ACT = mybir.ActivationFunctionType
ALU = mybir.AluOpType

HEADS, HEAD_DIM = 16, 64
PAIRS = HEADS // 2
D_FF = 2816
FF_CHUNKS = D_FF // (2 * P)
EPS = 1e-6
MASKED = -1e30
EXP_AND_LN = 6

CONV_TAPS = 31
RET_HEADS, RET_DIM = 4, 256
CHUNKS = T // P

TURN = 2.0 * np.pi
TURN_PARTS = (6.28125, 0.0019350051879882812, 3.019915981956753e-07)
ROUND = 1.5 * 2.0 ** 23
S5_TAU, S5_H, S5_N = 8, 16, 64
S5_GROUPS = D // S5_H
S5_PAIRS = S5_GROUPS // 2
S5_BLOCKS = T // S5_TAU
S5_RUN = 16
S5_RUNS = S5_BLOCKS // S5_RUN
SSD_HEADS, SSD_P, SSD_GROUPS, SSD_N = 16, 64, 4, 128
SSD_TAPS = 4

PHASES = [
    ("attn", PAIRS, 4, 22),
    ("ffn_first", 1, 8, 12), ("ffn", (FF_CHUNKS - 1) // 2, 16, 52), ("ffn_last", 1, 2, 16),
    ("side1", 1, 2, 16), ("gate1", 4, 2, 4),
    ("conv", KT, 4, 8), ("ret", RET_HEADS, 8, 28), ("pw", 4, 4, 20),
    ("s5_u", 4, 2, 4), ("s5_z", 4, 2, 4), ("ssd_z", 4, 2, 4), ("xbc", 8, 2, 4), ("dt", 1, 2, 2),
    ("ssd_out", 4, 2, 4), ("glu", 4, 4, 20),
    ("side3", 1, 2, 16), ("gate3", 4, 2, 4),
]
PANEL0, UNIT0 = {}, {}
_p = _u = 0
for _name, _n, _dp, _du in PHASES:
    PANEL0[_name], UNIT0[_name] = _p, _u
    _p, _u = _p + _n * _dp, _u + _n * _du
N_PANELS, N_UNITS = _p, _u
TURNS = {name: n for name, n, _, _ in PHASES}
PANELS = {name: n for name, _, n, _ in PHASES}
UNITS = {name: n for name, _, _, n in PHASES}

PANEL_UNITS = {
    "attn": [2, 4, 6, 22],
    "ffn_first": [2, 4, 6, 8, 9, 10, 11, 12],
    "ffn": [2, 4, 6, 8, 16, 24, 26, 28, 30, 32, 40, 48, 49, 50, 51, 52],
    "ffn_last": [8, 16], "side1": [8, 16], "side3": [8, 16],
    "conv": [2, 4, 6, 8],
    "ret": [2, 4, 6, 8, 10, 12, 20, 28],
    "pw": [2, 4, 12, 20], "glu": [2, 4, 12, 20],
    "dt": [2, 2],
}
for _name in ("gate1", "s5_u", "s5_z", "ssd_z", "xbc", "ssd_out", "gate3"):
    PANEL_UNITS[_name] = [2, 4]

COLS, _c = {}, 0
for _name, _n in [
    ("norm_mix", 8), ("norm_ffn", 8), ("norm_ple", 8), ("final_norm", 8),
    ("norm_g_2", 8), ("final_g_2", 8), ("norm_w_3", 8), ("ple_norm_w_3", 8), ("final_norm_w_3", 8),
    ("c_2", 8), ("ada_b_2", 24), ("conv_w_2", 8 * CONV_TAPS), ("conv_b_2", 8),
    ("conv_ln_g_2", 8), ("conv_ln_b_2", 8), ("ret_gn_g_2", 8), ("ret_gn_b_2", 8),
    ("conv_w_3", 16 * SSD_TAPS), ("conv_b_3", 16), ("s5_b_glu_3", 8), ("ssd_norm_w_3", 8),
    ("s5_D_3", S5_GROUPS), ("dt_bias_3", 16), ("A_log_3", 16), ("ssd_D_3", 16),
]:
    COLS[_name] = (_c, _n)
    _c += _n
N_COLS = _c
MATS = ["ones", "ident", "after", "upto", "masked"]


class Count:

    def __init__(self, i, c, b):
        self.i, self.c, self.b = i, c, b

    def __add__(self, n):
        return Count(self.i, self.c, self.b + n)

    def value(self, more=0):
        return self.b + more if self.i is None else self.i * self.c + (self.b + more)

    def half(self, more=0):
        if self.i is None:
            return self.b // 2 + more
        assert self.c % 2 == 0
        return self.i * (self.c // 2) + (self.b // 2 + more)


def units(name, i=None):
    return Count(i, UNITS[name], UNIT0[name])


def panels(name, i=None):
    return Count(i, PANELS[name], PANEL0[name])


def build(nc, ins, out, last=None):
    run = [n for n, *_ in PHASES]
    if last:
        run = run[:run.index(last) + 1]
    n_panels = PANEL0[run[-1]] + TURNS[run[-1]] * PANELS[run[-1]]
    ctx = ExitStack()
    with ctx:
        sems = {}

        def S(name):
            if name not in sems:
                sems[name] = ctx.enter_context(nc.semaphore(name))
            return sems[name]

        def sb(name, shape, dt=F32, stack=ctx):
            return stack.enter_context(nc.sbuf_tensor(name, shape, dt))

        def dram(name, shape):
            return nc.dram_tensor(name, shape, F32, kind="Internal").ap()

        banks = [ctx.enter_context(nc.psum_tensor(f"bank{b}", [P, 512], F32)) for b in range(8)]

        h = sb("h", [P, KT, T])
        xh = sb("xh", [P, KT, T], F32R)
        xl = sb("xl", [P, KT, T], F32R)
        raw = sb("raw", [P, 2, KT, P])
        wh = sb("wh", [P, 2, KT, P], F32R)
        wl = sb("wl", [P, 2, KT, P], F32R)
        cols = sb("cols", [P, N_COLS])
        mats = sb("mats", [P, len(MATS), P])
        mod = sb("mod", [P, 24])
        modg = sb("modg", [P, KT])
        cf = sb("cf", [P, KT, 2])
        ch = sb("ch", [P, KT, 2], F32R)
        cl = sb("cl", [P, KT, 2], F32R)
        eps = sb("eps", [P, 1])
        dt = sb("dt", [P, CHUNKS, SSD_HEADS])
        da = sb("da", [P, CHUNKS, SSD_HEADS])
        dtmp = sb("dtmp", [P, CHUNKS, SSD_HEADS])
        expA = sb("expA", [P, SSD_HEADS])
        dec = sb("dec", [P, 3, CHUNKS, SSD_HEADS])
        s5c = sb("s5c", [P, 12, S5_PAIRS])
        s5p = sb("s5p", [P, 2, S5_TAU + 1, S5_PAIRS])
        M = {name: mats[:, i, :] for i, name in enumerate(MATS)}

        def col(name, i, n=1):
            return cols[:, COLS[name][0] + i:COLS[name][0] + i + n]

        def norm_buffers(stack):
            sq = sb("sq", [P, 2, T], F32, stack)
            return dict(sq=sq, hn=sq, acc=sb("acc", [P, T], F32, stack), rinv=sb("rinv", [P, T], F32, stack))

        with ExitStack() as st:
            nb = norm_buffers(st)
        with ExitStack() as st:
            qT = sb("qT", [P, T], F32, st)
            kT = sb("kT", [P, T], F32, st)
            vtok = sb("vtok", [P, CHUNKS, P], F32, st)
            oh = sb("oh", [P, T], F32R, st)
            ol = sb("ol", [P, T], F32R, st)
            ub = sb("ub", [P, 2, 512], F32, st)
            lb = sb("lb", [P, 2, 512], F32, st)
            spb = sb("spb", [P, 4, 512], F32, st)
            wb = sb("wb", [P, 4, 512], F32, st)
            ab = sb("ab", [P, 4, 512], F32, st)
        with ExitStack() as st:
            pad_ = sb("pad_norms", [P, 4 * T], F32, st)
            gh = sb("gh", [P, 2, 2, T], F32R, st)
            gl = sb("gl", [P, 2, 2, T], F32R, st)
            sa = sb("sa", [P, 2, HALF], F32, st)
            gt = sb("gt", [P, 2, HALF], F32, st)
        with ExitStack() as st:
            sg = sb("sg", [P, 2, HALF], F32, st)
            pad_2 = sb("pad_norms2", [P, 3 * T], F32, st)
            pf = sb("pf", [P, 2, T], F32, st)
            ph = sb("ph", [P, 2, T], F32R, st)
            pl = sb("pl", [P, 2, T], F32R, st)
            side = sb("side", [P, KT, T], F32, st)

        with ExitStack() as st:
            apad = sb("apad", [P, T + CONV_TAPS - 1], F32, st)
            sigb = sb("sigb", [P, T], F32, st)
            cacc = sb("cacc", [P, 2, T], F32, st)
            cout = sb("cout", [P, T], F32, st)
            gates = sb("gates", [P, 2, T], F32, st)
        with ExitStack() as st:
            tabs = sb("tabs", [P, 4, T], F32, st)
            qr = sb("qr", [P, 2, T], F32, st)
            kr = sb("kr", [P, 2, T], F32, st)
            vt = sb("vt", [P, CHUNKS, 2 * P], F32, st)
            ot = sb("ot", [P, 2, T], F32, st)
            rh = sb("rh", [P, 2, T], F32R, st)
            rl = sb("rl", [P, 2, T], F32R, st)
            pt = sb("pt", [P, 2, HALF], F32, st)
            rt = sb("rt", [P, 2, HALF], F32, st)
            rg = tabs[:, 0:2, :]
        with ExitStack() as st:
            cg = sb("cg", [P, 2, T], F32, st)
            yt = sb("yt", [P, 2, HALF], F32, st)
            pad_3 = sb("pad_norms3", [P, T], F32, st)
            cv = sb("cv", [P, KT, T], F32, st)
            yh = sb("yh", [P, 2, T], F32R, st)
            yl = sb("yl", [P, 2, T], F32R, st)
        with ExitStack() as st:
            spill = sb("spill", [P, 2, T], F32, st)
            xc = sb("xc", [P, 2, T + SSD_TAPS - 1], F32, st)
        with ExitStack() as st:
            f = sb("f", [P, 2, 16, P], F32, st)
            zf = sb("zf", [P, 2, KT, P], F32, st)
            xt = sb("xt", [P, D], F32, st)
            bt = sb("bt", [P, SSD_GROUPS * P], F32, st)
            xd = sb("xd", [P, D], F32, st)
            xe = sb("xe", [P, D], F32, st)
            mt = sb("mt", [P, SSD_HEADS, P], F32, st)
            lt = sb("lt", [P, SSD_HEADS, P], F32, st)
            sm = sb("sm", [P, SSD_GROUPS, P], F32, st)
            ys = sb("ys", [P, D], F32, st)
            yd = sb("yd", [P, D], F32, st)
            state = sb("state", [P, D], F32, st)
            rs = sb("rs", [P, SSD_GROUPS, P], F32, st)
        with ExitStack() as st:
            s5t = sb("s5t", [P, 2, 4, S5_TAU, S5_H], F32, st)
            u5 = sb("u5", [P, S5_GROUPS, S5_BLOCKS], F32, st)
            s5 = sb("s5", [P, 2, S5_PAIRS, S5_BLOCKS], F32, st)
            pb = sb("pb", [P, 2, 4, S5_TAU, S5_H], F32, st)
            wz = sb("wz", [P, 2, 2, 4, P], F32, st)
            s5r = sb("s5r", [P, 2, S5_TAU, S5_PAIRS], F32, st)
            s5q = wz[:, 0, :, :, :].rearrange("p c q n -> p c (q n)").rearrange("p c (q j) -> p c q j", j=S5_RUN)
            w3 = sb("w3", [P, 8, S5_TAU, S5_H], F32, st)
            gm, b0, bm = [t[:, :, :].rearrange("p c h -> p (c h)") for t in (dtmp, da, dt)]
            gm = gm.rearrange("p (g h) -> p g h", g=8)
            b0, bm = [t.rearrange("p (c q h) -> p c q h", c=2, q=4) for t in (b0, bm)]
            bc = sb("bc", [P, 4, 4, S5_H], F32, st)
        with ExitStack() as st:
            y5 = sb("y5", [P, KT, T], F32, st)
            yg = sb("yg", [P, 2, T], F32, st)
            z5 = sb("z5", [P, 2, T], F32, st)
            sig5 = sb("sig5", [P, 2, HALF], F32, st)
            vt5 = sb("vt5", [P, 2, HALF], F32, st)
            vh = sb("vh", [P, 2, T], F32R, st)
            vl = sb("vl", [P, 2, T], F32R, st)
        gate_spill = dram("gate_spill", [2, KT, P, T])
        conv_spill = dram("conv_spill", [KT, P, T])
        spills = dram("spills", [3 * KT + 16, P, T])
        y_spill = dram("y_spill", [D, S5_TAU, S5_BLOCKS])
        wstream = ins["wstream"]
        block = ctx.enter_context(nc.Block())
        ret_steps = [(th, i) for th in range(2) for i in range(4 * th + 4)]
        ret_col = [max(0, i * P - th * HALF) for th, i in ret_steps]
        RS = len(ret_steps)
        ret_diag_no, n_ = [], 0
        for th, i in ret_steps:
            n_ += i >= 4 * th
            ret_diag_no.append(n_ if i >= 4 * th else 0)
        ret_rest_no, n_ = [], 0
        for s_, c0 in enumerate(ret_col):
            rest = not ret_diag_no[s_] or c0 + P < HALF
            n_ += rest
            ret_rest_no.append(n_ if rest else 0)
        ret_rest_no.append(n_)
        seg_banks = [2, 3, 7, 6]

        def settled(eng):
            eng.wait_ge(S("setup"), 64)

        def at(i, c, b):
            return Count(None, c, b) if isinstance(i, int) else Count(i, c, b)

        def turns(eng, n):
            yield 0
            with eng.Fori(1, n) as i:
                yield i

        def u_at(n, q):
            return n * 8 + q

        def s_at(n, p):
            return n * 4 + p

        steps = [(th, i, a) for th in range(2) for i in range(4 * th + 3, -1, -1) for a in range(2)]
        first_col = [max(0, i * P - th * HALF) for th, i, a in steps]
        cum1, cum2, n_cum = [], [], 0
        for s, (th, i, a) in enumerate(steps):
            n_cum += 1
            cum1.append(n_cum)
            n_cum += i > 0
            cum2.append(n_cum)
        NS = len(steps)

        def evicted(eng, unit):
            eng.wait_ge(S(f"bank_free{unit.b % 2}"), unit.half(1))

        def produced(eng, unit):
            eng.wait_ge(S("unit_done"), unit.value(1))

        def all_evicted(eng, name):
            for b in range(2):
                eng.wait_ge(S(f"bank_free{b}"), (UNIT0[name] + TURNS[name] * UNITS[name]) // 2)

        @block.sync
        def _(sp):
            for s in range(2):
                sp.dma_start(raw[:, s].rearrange("p k n -> p (k n)"), wstream[s]).then_inc(S(f"panel_in{s}"), 16)
            with sp.Fori(1, n_panels // 2) as i:
                for s in range(2):
                    sp.wait_ge(S("panel_split"), i * 2 + s - 1)
                    sp.dma_start(raw[:, s].rearrange("p k n -> p (k n)"), wstream[i * 2 + s]).then_inc(
                        S(f"panel_in{s}"), 16)
            sp.wait_ge(S("stored"), 128)

        @block.gpsimd
        def _(pool):
            nc.gpsimd.memset(eps[:, :], EPS).then_inc(S("eps"), 1)
            ones = M["ones"].unsqueeze(1).broadcast_to([P, KT, P])
            pool.wait_ge(S("setup"), 64)

            def split(panel, freed):
                slot = panel.b % 2
                pool.wait_ge(S(f"panel_in{slot}"), panel.half(1) * 16)
                if freed is not None:
                    pool.wait_ge(S("unit_done"), freed.value())
                nc.gpsimd.tensor_tensor(wh[:, slot], raw[:, slot], ones, ALU.mult).then_inc(S("panel_high"), 1)
                pool.wait_ge(S("panel_high"), panel.value(1))
                nc.gpsimd.tensor_tensor(wl[:, slot], raw[:, slot], wh[:, slot].bitcast(F32),
                                        ALU.subtract).then_inc(S("panel_split"), 1)

            def turn(name, i, before):
                for m in range(PANELS[name]):
                    split(panels(name, i) + m, before[m] if m < 2 else units(name, i) + PANEL_UNITS[name][m - 2])

            before = [None, None]
            for name in run:
                n, dp = TURNS[name], PANELS[name]
                assert dp % 2 == 0 and PANEL0[name] % 2 == 0
                turn(name, None, before)
                if n > 1:
                    with pool.Fori(1, n) as i:
                        turn(name, i, [units(name, i) + (PANEL_UNITS[name][dp - 2 + m] - UNITS[name])
                                       for m in range(2)])
                before = [units(name) + ((n - 1) * UNITS[name] + PANEL_UNITS[name][dp - 2 + m]) for m in range(2)]

        @block.tensor
        def _(pe):
            def mm3(o, lh, ll, rh, rl, start, stop):
                nc.tensor.matmul(o, lh, rh, start=start, stop=False)
                nc.tensor.matmul(o, lh, rl, start=False, stop=False)
                return nc.tensor.matmul(o, ll, rh, start=False, stop=stop)

            def bank_free(unit):
                if unit.i is not None or unit.b >= 2:
                    pe.wait_ge(S(f"bank_free{unit.b % 2}"), unit.half())

            def split_done(panel):
                pe.wait_ge(S("panel_split"), panel.value(1))

            def tile(unit, slot, slabs, rhs):
                for th in range(2):
                    bank_free(unit + th)
                    for n, (slab, (rh, rl)) in enumerate(zip(slabs, rhs)):
                        t = slice(th * HALF, (th + 1) * HALF)
                        mm = mm3(banks[th][:, :], wh[:, slot, slab, :], wl[:, slot, slab, :],
                                 rh[:, t], rl[:, t], n == 0, n == len(slabs) - 1)
                    mm.then_inc(S("unit_done"), 1)

            def tile_x(unit, panel):
                split_done(panel)
                tile(unit, panel.b % 2, range(KT), [(xh[:, k, :], xl[:, k, :]) for k in range(KT)])

            def tile_tokens(unit, panel, width=P, per_bank=4):
                split_done(panel)
                slot = panel.b % 2
                for th in range(2):
                    bank_free(unit + th)
                    for q in range(4):
                        t = slice((4 * th + q) * P, (4 * th + q + 1) * P)
                        for k in range(KT):
                            mm = mm3(banks[th][:, q * width:(q + 1) * width], xh[:, k, t], xl[:, k, t],
                                     wh[:, slot, k, :width], wl[:, slot, k, :width], k == 0, k == KT - 1)
                    mm.then_inc(S("unit_done"), 1)

            def norm_sums(n):
                pe.wait_ge(S("norm_acc"), n * KT + KT)
                if n:
                    pe.wait_ge(S("norm_root"), 2 * n)
                for th in range(2):
                    nc.tensor.matmul(banks[2 + th][:, :], M["ones"], nb["acc"][:, th * HALF:(th + 1) * HALF],
                                     start=True, stop=True).then_inc(S("norm_sum"), 1)

            def out_two(unit, panel, high, low):
                for n in range(KT):
                    if n % 4 == 0:
                        split_done(panel + n // 4)
                    tile(unit + 2 * n, (panel.b + n // 4) % 2, [2 * (n % 4), 2 * (n % 4) + 1],
                         [(high[:, t, :], low[:, t, :]) for t in range(2)])

            def modulation(unit, panel):
                split_done(panel)
                bank_free(unit)
                for k in range(KT):
                    mm = mm3(banks[unit.b % 2][:, 0:2], wh[:, panel.b % 2, k, :], wl[:, panel.b % 2, k, :],
                             ch[:, k, :], cl[:, k, :], k == 0, k == KT - 1)
                mm.then_inc(S("unit_done"), 1)

            pe.wait_ge(S("setup"), 64)
            norm_sums(0)
            pe.wait_ge(S("norm_low"), KT)
            with pe.Fori(0, PAIRS) as j:
                unit, panel = units("attn", j), panels("attn", j)
                tile_x(unit, panel)
                tile_x(unit + 2, panel + 1)
                tile_tokens(unit + 4, panel + 2)
                evicted(pe, unit + 4)
                evicted(pe, unit + 5)

                def scores(s):
                    th, i, a = steps[s]
                    c0 = first_col[s]
                    diagonal = i >= 4 * th
                    if s >= 2:
                        pe.wait_ge(S("w_ready"), j * NS + (s - 1))
                    rows = slice(a * HEAD_DIM, (a + 1) * HEAD_DIM)
                    z = banks[4 + s % 2]
                    mm = nc.tensor.matmul(z[:, c0:], kT[rows, i * P:(i + 1) * P],
                                          qT[rows, th * HALF + c0:(th + 1) * HALF], start=True, stop=True)
                    if diagonal:
                        mm = nc.tensor.matmul(z[:, c0:c0 + P], M["ident"], M["masked"], start=False, stop=True,
                                              skip_group_check=True)
                    mm.then_inc(S("scores_ready"), 1)

                def cumulate(s):
                    th, i, a = steps[s]
                    c0 = first_col[s]
                    pe.wait_ge(S("sp_ready"), j * NS + (s + 1))
                    if i == 4 * th + 3 and th:
                        pe.wait_ge(S("e_ready"), j * NS + (s - 1))
                    nc.tensor.matmul(banks[6 + a][:, c0:], M["after"], spb[:, s % 4, c0:], start=i == 4 * th + 3,
                                     stop=True, skip_group_check=True).then_inc(S("cum_done"), 1)

                def carry(s):
                    th, i, a = steps[s]
                    c0 = first_col[s]
                    if i:
                        pe.wait_ge(S("e_ready"), j * NS + (s + 1))
                        nc.tensor.matmul(banks[6 + a][:, c0:], M["upto"], spb[:, s % 4, c0:], start=False,
                                         stop=True, skip_group_check=True).then_inc(S("cum_done"), 1)

                def values(s):
                    th, i, a = steps[s]
                    c0 = first_col[s]
                    pe.wait_ge(S("a_ready"), j * NS + (s + 1))
                    rows = slice(a * HEAD_DIM, (a + 1) * HEAD_DIM)
                    nc.tensor.matmul(banks[2 + th][rows, c0:], vtok[:, i, rows], ab[:, s % 4, c0:],
                                     start=i == 4 * th + 3, stop=i == 0, skip_group_check=True
                                     ).then_inc(S("value_done"), 1)

                scores(0)
                scores(1)
                for s in range(NS + 2):
                    if s < NS:
                        cumulate(s)
                    if s + 2 < NS:
                        scores(s + 2)
                    if s >= 2:
                        values(s - 2)
                    if s < NS:
                        carry(s)
                split_done(panel + 3)
                pe.wait_ge(S("ol_ready"), j * 2 + 2)
                for n in range(KT):
                    tile(unit + (6 + 2 * n), 1, [n], [(oh[:, :], ol[:, :])])

            if "ffn_first" in run:
                norm_sums(1)
                pe.wait_ge(S("norm_low"), 2 * KT)

                def hidden(unit, panel):
                    for m in range(4):
                        tile_x(unit + 2 * m, panel + m)

                hidden(units("ffn_first"), panels("ffn_first"))
                pe.wait_ge(S("cl_ready"), 1)
                for m in range(4):
                    modulation(units("ffn_first") + (8 + m), panels("ffn_first") + (4 + m))
                with pe.Fori(0, TURNS["ffn"]) as i:
                    unit, panel = units("ffn", i), panels("ffn", i)
                    hidden(unit, panel)
                    pe.wait_ge(S("gl_ready"), i * 8 + 4)
                    out_two(unit + 8, panel + 4, gh[:, 0], gl[:, 0])
                    hidden(unit + 24, panel + 6)
                    pe.wait_ge(S("gl_ready"), i * 8 + 8)
                    out_two(unit + 32, panel + 10, gh[:, 1], gl[:, 1])
                    for m in range(4):
                        modulation(unit + (48 + m), panel + (12 + m))
                pe.wait_ge(S("gl_ready"), 4 * FF_CHUNKS)
                out_two(units("ffn_last"), panels("ffn_last"), gh[:, 0], gl[:, 0])

            def side_product(name, n):
                pe.wait_ge(S("pl_ready"), n)
                for m in range(KT):
                    if m % 4 == 0:
                        split_done(panels(name) + m // 4)
                    tile(units(name) + 2 * m, m // 4, [2 * (m % 4), 2 * (m % 4) + 1],
                         [(ph[:, t, :], pl[:, t, :]) for t in range(2)])

            def plain(name):
                with pe.Fori(0, TURNS[name]) as i:
                    for m in range(2):
                        tile_x(units(name, i) + 2 * m, panels(name, i) + m)

            if "side1" in run:
                side_product("side1", 1)
            if "gate1" in run:
                norm_sums(2)
                pe.wait_ge(S("norm_low"), 3 * KT)
                plain("gate1")
                norm_sums(3)
            if "conv" in run:
                norm_sums(4)
                pe.wait_ge(S("norm_low"), 4 * KT)
                with pe.Fori(0, KT) as i:
                    for m in range(4):
                        tile_x(units("conv", i) + 2 * m, panels("conv", i) + m)

            def retention(i):
                unit, panel = units("ret", i), panels("ret", i)
                n = 0 if i is None else i
                for m in range(4):
                    tile_x(unit + 2 * m, panel + m)
                for m in range(2):
                    tile_tokens(unit + (8 + 2 * m), panel + (4 + m))
                evicted(pe, unit + 10)
                evicted(pe, unit + 11)
                pe.wait_ge(S("rope_done"), n * 8 + 8)

                def probs_ready(s):
                    if ret_rest_no[s]:
                        pe.wait_ge(S("p_rest"), n * ret_rest_no[-1] + ret_rest_no[s])
                    if ret_diag_no[s]:
                        pe.wait_ge(S("p_diag"), n * 8 + ret_diag_no[s])

                def scores(s):
                    th, i = ret_steps[s]
                    c0 = ret_col[s]
                    if s >= 2:
                        probs_ready(s - 2)
                    for k in range(2):
                        mm = nc.tensor.matmul(banks[4 + s % 2][:, c0:], kr[:, k, i * P:(i + 1) * P],
                                              qr[:, k, th * HALF + c0:(th + 1) * HALF], start=k == 0, stop=k == 1)
                    mm.then_inc(S("ret_scores"), 1)

                def values(s):
                    th, i = ret_steps[s]
                    c0 = ret_col[s]
                    probs_ready(s)
                    if i == 0 and th:
                        pe.wait_ge(S("o_ready"), n * 4 + 2)
                    for m in range(2):
                        mm = nc.tensor.matmul(banks[6 + m][:, c0:], vt[:, i, m * P:(m + 1) * P],
                                              pt[:, s % 2, c0:], start=i == 0, stop=i == 4 * th + 3,
                                              skip_group_check=True)
                    mm.then_inc(S("ret_values"), 1)

                scores(0)
                for s in range(RS):
                    if s + 1 < RS:
                        scores(s + 1)
                    values(s)
                for r, (sem, count, src) in enumerate((("o_ready", 4, ot), ("o_square", 2, qr))):
                    pe.wait_ge(S(sem), n * count + count)
                    for th in range(2):
                        for m in range(2):
                            mm = nc.tensor.matmul(banks[2 + th][:, :], M["ones"],
                                                  src[:, m, th * HALF:(th + 1) * HALF], start=m == 0, stop=m == 1)
                        mm.then_inc(S("ret_sum"), 1)
                pe.wait_ge(S("rl_ready"), n + 1)
                out_two(unit + 12, panel + 6, rh, rl)

            if "ret" in run:
                retention(None)
                with pe.Fori(1, RET_HEADS) as i:
                    retention(i)

            def hidden_and_out(name, high, low, sem):
                with pe.Fori(0, 4) as i:
                    unit, panel = units(name, i), panels(name, i)
                    for m in range(2):
                        tile_x(unit + 2 * m, panel + m)
                    pe.wait_ge(S(sem), i * 4 + 4)
                    out_two(unit + 4, panel + 2, high, low)

            if "pw" in run:
                pe.wait_ge(S("mean_acc"), KT)
                for th in range(2):
                    nc.tensor.matmul(banks[2 + th][:, :], M["ones"], nb["acc"][:, th * HALF:(th + 1) * HALF],
                                     start=True, stop=True).then_inc(S("mean_sum"), 1)
                norm_sums(5)
                pe.wait_ge(S("norm_low"), 5 * KT)
                hidden_and_out("pw", yh, yl, "yl_ready")
                norm_sums(6)
            if "s5_u" in run:
                norm_sums(7)
                pe.wait_ge(S("norm_low"), 6 * KT)
                plain("s5_u")
                plain("s5_z")
                plain("ssd_z")
                plain("xbc")
                tile_tokens(units("dt"), panels("dt"), SSD_HEADS)
                pe.wait_ge(S("da_ready"), 1)
                for r, name in enumerate(("upto", "after", "ones")):
                    mm = nc.tensor.matmul(banks[2][:, r * P:(r + 1) * P], M[name],
                                          da[:, :, :].rearrange("p c h -> p (c h)"), start=True, stop=True)
                mm.then_inc(S("dec_sum"), 1)

            def ssd(c, b):
                F, g4 = f[:, b], range(SSD_GROUPS)
                pe.wait_ge(S(f"f_in{b}"), c.half(1) * 32)
                if c.i is not None or c.b > 0:
                    pe.wait_ge(S("ssd_low"), c.value())
                for q in range(8):
                    mm = nc.tensor.transpose(banks[4 + q // 4][:, q % 4 * P:(q % 4 + 1) * P], F[:, q, :], M["ident"])
                mm.then_inc(S("x_turned"), 1)
                for q in g4:
                    mm = nc.tensor.transpose(banks[6][:, q * P:(q + 1) * P], F[:, 8 + q, :], M["ident"])
                mm.then_inc(S("b_turned"), 1)
                pe.wait_ge(S("mt_ready"), c.value(1))
                for q in range(4):
                    if q == 3:
                        pe.wait_ge(S("bt_ready"), c.value(1))
                    nc.tensor.matmul(banks[seg_banks[q]][:, :], M["after"],
                                     mt[:, 4 * q:4 * q + 4, :].rearrange("p h t -> p (h t)"),
                                     start=True, stop=True).then_inc(S("seg_done"), 1)
                pe.wait_ge(S("xt_ready"), c.value(1))
                pe.wait_ge(S("xd_ready"), c.value(1))
                for g in g4:
                    mm = nc.tensor.matmul(banks[4][:, g * P:(g + 1) * P], F[:, 8 + g, :], F[:, 12 + g, :],
                                          start=True, stop=True)
                mm.then_inc(S("bc_done"), 1)
                pe.wait_ge(S("w_masked"), c.value(1))
                for hd in range(SSD_HEADS):
                    mm = nc.tensor.matmul(banks[2 + hd // 8][:, hd % 8 * SSD_P:(hd % 8 + 1) * SSD_P], lt[:, hd, :],
                                          xd[:, hd * SSD_P:(hd + 1) * SSD_P], start=True, stop=True)
                mm.then_inc(S("intra_done"), 1)
                pe.wait_ge(S("state_ready"), c.value(1))
                for g in g4:
                    mm = nc.tensor.matmul(banks[4 + g // 2][:, g % 2 * 256:(g % 2 + 1) * 256], F[:, 12 + g, :],
                                          state[:, g * 256:(g + 1) * 256], start=True, stop=True)
                mm.then_inc(S("inter_done"), 1)
                pe.wait_ge(S("xe_ready"), c.value(1))
                for g in g4:
                    mm = nc.tensor.matmul(banks[6 + g // 2][:, g % 2 * 256:(g % 2 + 1) * 256],
                                          bt[:, g * P:(g + 1) * P], xe[:, g * 256:(g + 1) * 256],
                                          start=True, stop=True)
                mm.then_inc(S("new_done"), 1)
                pe.wait_ge(S("ys_ready"), c.value(1))
                for q in range(8):
                    mm = nc.tensor.transpose(banks[4 + q // 4][:, q % 4 * P:(q % 4 + 1) * P],
                                             ys[:, q * P:(q + 1) * P], M["ident"])
                mm.then_inc(S("y_turned"), 1)
                pe.wait_ge(S("ssd_square"), c.value(1))
                pe.wait_ge(S("state_ready"), c.value(2))
                for g in g4:
                    for m in range(2):
                        mm = nc.tensor.matmul(banks[6][:, g * P:(g + 1) * P], M["ones"],
                                              xe[:, (2 * g + m) * P:(2 * g + m + 1) * P], start=m == 0, stop=m == 1)
                mm.then_inc(S("ssd_sum"), 1)

            if "ssd_out" in run:
                pe.wait_ge(S("dec_ready"), 1)
                for i in turns(pe, CHUNKS // 2):
                    for b in range(2):
                        ssd(at(i, 2, b), b)
                pe.wait_ge(S("ssd_low"), CHUNKS)
                plain("ssd_out")

            def s5_inputs(n):
                pe.wait_ge(S("pb_ready"), n + 1)
                if not isinstance(n, int):
                    pe.wait_ge(S("s5_stored"), n)
                    pe.wait_ge(S("s5_local_added"), n)
                settled(pe)
                for c in range(2):
                    for p in range(4):
                        mm = nc.tensor.transpose(banks[2 + c][:, p * P:(p + 1) * P], pb[:, c, p, :, :], M["ident"])
                mm.then_inc(S("w1_turned"), 1)
                for p in range(4):
                    for par in range(2):
                        rows = slice(par * S5_N, (par + 1) * S5_N)
                        for c in range(2):
                            mm = nc.tensor.matmul(banks[6 + par][:, p * S5_H:(p + 1) * S5_H],
                                                  pb[rows, c, p, :, :], bm[rows, c, p, :], start=c == 0, stop=c == 1)
                mm.then_inc(S("gm_done"), 1)
                pe.wait_ge(S("w1_ready"), n + 1)
                settled(pe)
                for p in range(4):
                    for par in range(2):
                        for c in range(2):
                            mm = nc.tensor.matmul(banks[4 + c][:, p * P:(p + 1) * P], wz[:, par, c, p, :],
                                                  u5[:, u_at(n, 2 * p + par), :], start=par == 0, stop=par == 1,
                                                  skip_group_check=True)
                mm.then_inc(S("s5_in"), 1)
                pe.wait_ge(S("w3_in"), n * 128 + 128)
                pe.wait_ge(S("gm_ready"), n + 1)
                settled(pe)
                for q in range(8):
                    mm = nc.tensor.matmul(banks[6 + q // 4][:, q % 4 * P:(q % 4 + 1) * P], w3[:, q, :, :],
                                          u5[:, u_at(n, q), :], start=True, stop=True)
                mm.then_inc(S("s5_local"), 1)

            def s5_outputs(n):
                pe.wait_ge(S("wc_ready"), n + 1)
                if not isinstance(n, int):
                    pe.wait_ge(S("s5_added"), n)
                settled(pe)
                for q in range(8):
                    p = q // 2
                    for c in range(2):
                        mm = nc.tensor.matmul(banks[4 + q // 4][:, q % 4 * P + 1:(q % 4 + 1) * P],
                                              wz[:, q % 2, c, p, :], s5[:, c, s_at(n, p), 0:S5_BLOCKS - 1],
                                              start=c == 0, stop=c == 1)
                mm.then_inc(S("s5_carried"), 1)

            if "glu" in run:
                pe.wait_ge(S("u5_in"), S5_TAU * 16)
                pe.wait_ge(S("w3_zero"), 1)
                for i in turns(pe, KT):
                    s5_inputs(i)
                pe.wait_ge(S("s5_scan"), 5 * (S5_RUN - 1 + S5_RUNS - 1))
                for i in turns(pe, KT):
                    s5_outputs(i)
                pe.wait_ge(S("yg_low"), KT)
                hidden_and_out("glu", vh, vl, "vl_ready")
                side_product("side3", 2)
            if "gate3" in run:
                norm_sums(8)
                pe.wait_ge(S("norm_low"), 7 * KT)
                plain("gate3")
                norm_sums(9)

        @block.scalar
        def _(act):
            A = nc.scalar.activation

            def load_functions(table_set):
                act.add_instruction(mybir.InstLoadActFuncSet(
                    name=nc.get_next_instruction_name(), act_func_set_id=table_set, engine=act.engine,
                    ins=[], outs=[]))

            def norm(n, sn, mode="split", src=h):
                hn = nb["hn"]
                for k in range(KT):
                    if k >= 2:
                        act.wait_ge(S("norm_acc"), n * KT + k - 1)
                    A(nb["sq"][:, k % 2, :], src[:, k, :], ACT.Square).then_inc(S("norm_square"), 1)
                for th in range(2):
                    act.wait_ge(S("norm_sum"), 2 * n + th + 1)
                    A(nb["rinv"][:, th * HALF:(th + 1) * HALF], banks[2 + th][:, :], ACT.Sqrt,
                      bias=eps[:, 0:1], scale=1.0 / D).then_inc(S("norm_root"), 1)
                if mode == "keep":
                    return
                for k in range(KT):
                    act.wait_ge(S("norm_scaled"), n * KT + k + 1)
                    if mode == "mod":
                        A(xh[:, k, :], hn[:, k % 2, :], ACT.Identity, bias=mod[:, k:k + 1]
                          ).then_inc(S("norm_high"), 1)
                        continue
                    if mode == "silu":
                        A(hn[:, k % 2, :], hn[:, k % 2, :], ACT.Silu, bias=col("conv_ln_b_2", k)
                          ).then_inc(S("norm_silu"), 1)
                        act.wait_ge(S("norm_silu"), k + 1)
                    A(xh[:, k, :], hn[:, k % 2, :], ACT.Copy).then_inc(S("norm_high"), 1)

            act.dma_start(cols[:, :], ins["cols"]).then_inc(S("setup"), 16)
            act.dma_start(mats[:, :, :], ins["mats"]).then_inc(S("setup"), 16)
            for k in range(0, KT, 4):
                act.dma_start(h[:, k:k + 4, :], ins["x"][:, k:k + 4, :]).then_inc(S("setup"), 16)
            act.dma_start(s5c[:, 0:3, :], ins["s5_small"]).then_inc(S("s5_small_in"), 16)
            act.wait_ge(S("eps"), 1)
            act.wait_ge(S("setup"), 64)
            norm(0, 0)
            for m in range(2):
                A(cf[:, :, m], col("c_2", 0, KT), ACT.Silu).then_inc(S("cf_ready"), 1)
            act.wait_ge(S("cf_ready"), 2)
            A(ch[:, :, :], cf[:, :, :], ACT.Copy).then_inc(S("ch_ready"), 1)

            load_functions(EXP_AND_LN)
            with act.Fori(0, PAIRS) as j:
                unit = units("attn", j)
                for th in range(2):
                    produced(act, unit + th)
                    A(qT[:, th * HALF:(th + 1) * HALF], banks[th][:, :], ACT.Copy, scale=HEAD_DIM ** -0.5
                      ).then_inc(S(f"bank_free{th}"), 1)
                for th in range(2):
                    produced(act, unit + (4 + th))
                    A(vtok[:, 4 * th:4 * th + 4, :], banks[th][:, :].rearrange("p (c n) -> p c n", n=P), ACT.Copy
                      ).then_inc(S(f"bank_free{th}"), 1)

                def soft(s):
                    c0, b = first_col[s], s % 2
                    act.wait_ge(S("scores_ready"), j * NS + (s + 1))
                    A(ub[:, b, c0:], banks[4 + b][:, c0:], ACT.Abs).then_inc(S("abs_done"), 1)
                    act.wait_ge(S("abs_done"), j * NS + (s + 1))
                    A(ub[:, b, c0:], ub[:, b, c0:], ACT.Exp, scale=-1.0).then_inc(S("exp_done"), 1)
                    act.wait_ge(S("exp_done"), j * NS + (s + 1))
                    if s >= 2:
                        act.wait_ge(S("w_ready"), j * NS + (s - 1))
                    A(lb[:, b, c0:], ub[:, b, c0:], ACT.Ln, bias=1.0).then_inc(S("log_ready"), 1)

                def weights(s):
                    c0 = first_col[s]
                    act.wait_ge(S("e_ready"), j * NS + (s + 1))
                    if s >= 4:
                        act.wait_ge(S("value_done"), j * NS + (s - 3))
                    A(ab[:, s % 4, c0:], wb[:, s % 4, c0:], ACT.Exp).then_inc(S("a_ready"), 1)

                for s in range(NS + 2):
                    if s < NS:
                        soft(s)
                    if s >= 2:
                        weights(s - 2)
                for th in range(2):
                    act.wait_ge(S("value_done"), j * NS + (8 if th == 0 else NS))
                    A(oh[:, th * HALF:(th + 1) * HALF], banks[2 + th][:, :], ACT.Copy).then_inc(S("oh_ready"), 1)

            if "ffn_first" in run:
                all_evicted(act, "attn")
                norm(1, 1)

                def hidden(unit, gh_before, parity):
                    for m in range(2):
                        for th in range(2):
                            produced(act, unit + (4 * m + th))
                            A(sa[:, th, :], banks[th][:, :], ACT.Silu).then_inc(S(f"bank_free{th}"), 1)
                        for th in range(2):
                            evicted(act, unit + (4 * m + 2 + th))
                            A(gh[:, parity, m, th * HALF:(th + 1) * HALF], gt[:, th, :], ACT.Copy
                              ).then_inc(S("gh_ready"), 1)

                hidden(units("ffn_first"), 0, 0)
                with act.Fori(0, TURNS["ffn"]) as i:
                    hidden(units("ffn", i), 0, 1)
                    hidden(units("ffn", i) + 24, 0, 0)

            def side_take(name, src, n):
                act.dma_start(pf[:, :, :], src).then_inc(S("side_in"), 16)
                act.wait_ge(S("side_in"), 16 * n)
                A(ph[:, :, :], pf[:, :, :], ACT.Copy).then_inc(S("ph_ready"), 1)
                for m in range(2 * KT):
                    th = m % 2
                    produced(act, units(name) + m)
                    A(side[:, m // 2, th * HALF:(th + 1) * HALF], banks[th][:, :], ACT.Copy
                      ).then_inc(S(f"bank_free{th}"), 1)

            def gate_take(name, g):
                for m in range(2 * KT):
                    produced(act, units(name) + m)
                    if m >= 2:
                        act.wait_ge(S("h_added"), 16 * g + m - 1)
                    A(sg[:, m % 2, :], banks[m % 2][:, :], ACT.Sigmoid).then_inc(S(f"bank_free{m % 2}"), 1)

            if "side1" in run:
                all_evicted(act, "ffn_last")
                side_take("side1", ins["p1"], 1)
            if "gate1" in run:
                all_evicted(act, "side1")
                norm(2, 2)
                gate_take("gate1", 0)
                act.wait_ge(S("h_added"), 16)
                norm(3, None, "keep")
            if "conv" in run:
                act.wait_ge(S("norm_scaled"), 4 * KT)
                norm(4, 3, "mod")

            def convolution(i):
                unit, n = units("conv", i), 0 if i is None else i
                for th in range(2):
                    produced(act, unit + th)
                    A(sigb[:, th * HALF:(th + 1) * HALF], banks[th][:, :], ACT.Sigmoid
                      ).then_inc(S(f"bank_free{th}"), 1)
                if i is not None:
                    act.wait_ge(S("conv_done"), n)
                    act.dma_start(conv_spill[n - 1], cout[:, :]).then_inc(S("conv_stored"), 16)
                    act.wait_ge(S("gates_stored"), n * 32)
                for m in range(2):
                    for th in range(2):
                        produced(act, unit + (4 + 2 * m + th))
                        A(gates[:, m, th * HALF:(th + 1) * HALF], banks[th][:, :], ACT.Silu
                          ).then_inc(S(f"bank_free{th}"), 1)
                    for th in range(2):
                        evicted(act, unit + (4 + 2 * m + th))
                    act.dma_start(gate_spill[m, n], gates[:, m, :]).then_inc(S("gates_stored"), 16)

            if "conv" in run:
                convolution(None)
                with act.Fori(1, KT) as i:
                    convolution(i)
                act.wait_ge(S("conv_done"), KT)
                act.dma_start(conv_spill[KT - 1], cout[:, :]).then_inc(S("conv_stored"), 16)

            def retention(i):
                unit, n = units("ret", i), 0 if i is None else i
                if i is not None:
                    act.wait_ge(S("ry_done"), n * 2)
                act.dma_start(tabs[:, :, :], ins["rope"][n]).then_inc(S("tabs_in"), 16)
                for m in range(2):
                    for th in range(2):
                        produced(act, unit + (8 + 2 * m + th))
                        A(vt[:, 4 * th:4 * th + 4, m * P:(m + 1) * P],
                          banks[th][:, :].rearrange("p (c n) -> p c n", n=P), ACT.Copy
                          ).then_inc(S(f"bank_free{th}"), 1)
                act.wait_ge(S("rope_done"), n * 8 + 8)
                act.dma_start(rg, gate_spill[1, bass.ds(n * 2, 2)].rearrange("k p t -> p k t")
                              if i is not None else gate_spill[1, 0:2].rearrange("k p t -> p k t")
                              ).then_inc(S("rg_in"), 16)
                for s, (th, j) in enumerate(ret_steps):
                    if ret_rest_no[s]:
                        c0 = ret_col[s] + (P if ret_diag_no[s] else 0)
                        act.wait_ge(S("ret_scores"), n * RS + (s + 1))
                        if ret_diag_no[s]:
                            act.wait_ge(S("p_diag"), n * 8 + ret_diag_no[s])
                        if s >= 2:
                            act.wait_ge(S("ret_values"), n * RS + (s - 1))
                        A(pt[:, s % 2, c0:], banks[4 + s % 2][:, c0:], ACT.Copy).then_inc(S("p_rest"), 1)
                    if j == 4 * th + 3:
                        act.wait_ge(S("ret_values"), n * RS + (s + 1))
                        for m in range(2):
                            A(ot[:, m, th * HALF:(th + 1) * HALF], banks[6 + m][:, :], ACT.Copy
                              ).then_inc(S("o_ready"), 1)
                act.wait_ge(S("o_centered"), n * 4 + 4)
                for m in range(2):
                    A(qr[:, m, :], ot[:, m, :], ACT.Square).then_inc(S("o_square"), 1)
                for th in range(2):
                    act.wait_ge(S("ret_sum"), n * 4 + (3 + th))
                    A(rt[:, th, :], banks[2 + th][:, :], ACT.Sqrt, bias=eps[:, 0:1], scale=1.0 / RET_DIM
                      ).then_inc(S("r_root"), 1)
                for m in range(2):
                    act.wait_ge(S("ry_done"), n * 2 + (m + 1))
                    A(rh[:, m, :], ot[:, m, :], ACT.Copy).then_inc(S("rh_ready"), 1)

            if "ret" in run:
                act.wait_ge(S("conv_stored"), KT * 16)
                act.wait_ge(S("gates_stored"), 2 * KT * 16)
                all_evicted(act, "conv")
                retention(None)
                with act.Fori(1, RET_HEADS) as i:
                    retention(i)

            if "pw" in run:
                all_evicted(act, "ret")
                act.dma_start(cv[:, :, :], conv_spill.rearrange("k p t -> p k t")).then_inc(S("cv_in"), 16)
                act.wait_ge(S("ln_centered"), 2 * KT)
                norm(5, 4, "silu", cv)
                act.wait_ge(S("norm_low"), 5 * KT)
                with act.Fori(0, 4) as i:
                    unit = units("pw", i)
                    for b in range(2):
                        act.wait_ge(S(f"bank_free{b}"), unit.half())
                    act.dma_start(cg[:, :, :], gate_spill[0, bass.ds(i * 2, 2)].rearrange("k p t -> p k t")
                                  ).then_inc(S("cg_in"), 16)
                    for m in range(2):
                        for th in range(2):
                            evicted(act, unit + (2 * m + th))
                            A(yh[:, m, th * HALF:(th + 1) * HALF], yt[:, th, :], ACT.Copy
                              ).then_inc(S("yh_ready"), 1)
                all_evicted(act, "pw")
                norm(6, None, "keep")

            def spill_tiles(name, first, func, permuted=False):
                for i in turns(act, 4):
                    n = i
                    unit = units(name, None if isinstance(i, int) else i)
                    for m in range(2):
                        before = first // 2 + n if isinstance(n, int) else n + first // 2
                        if not (isinstance(n, int) and before == 0):
                            act.wait_ge(S(f"spilled{m}"), before * 16)
                        for th in range(2):
                            produced(act, unit + (2 * m + th))
                            o, b = spill[:, m, th * HALF:(th + 1) * HALF], banks[th][:, :]
                            if permuted:
                                q = S5_BLOCKS // 2
                                o = spill[:, m, :].rearrange("p (t b) -> p b t", t=S5_TAU)[:, th * q:(th + 1) * q, :]
                                b = b.rearrange("p (b t) -> p b t", t=S5_TAU)
                            A(o, b, func).then_inc(S(f"bank_free{th}"), 1)
                        for th in range(2):
                            evicted(act, unit + (2 * m + th))
                        act.dma_start(spills[n * 2 + (first + m)], spill[:, m, :]).then_inc(S(f"spilled{m}"), 16)

            if "s5_u" in run:
                act.wait_ge(S("norm_scaled"), 7 * KT)
                norm(7, 5)
                spill_tiles("s5_u", 0, ACT.Copy, True)
                spill_tiles("s5_z", KT, ACT.Silu)
                spill_tiles("ssd_z", 2 * KT, ACT.Silu)
                for i in turns(act, KT):
                    n, unit = i, units("xbc", None if isinstance(i, int) else i)
                    for m in range(2):
                        if not isinstance(i, int):
                            act.wait_ge(S("xo_ready"), n * 2 + (m - 1))
                        for th in range(2):
                            produced(act, unit + (2 * m + th))
                            A(xc[:, m, SSD_TAPS - 1 + th * HALF:SSD_TAPS - 1 + (th + 1) * HALF], banks[th][:, :],
                              ACT.Copy).then_inc(S(f"bank_free{th}"), 1)
                    for m in range(2):
                        act.wait_ge(S("xo_ready"), n * 2 + (m + 1))
                        A(spill[:, m, :], spill[:, m, :], ACT.Silu).then_inc(S("xs_ready"), 1)
                        act.wait_ge(S("xs_ready"), n * 2 + (m + 1))
                        act.dma_start(spills[n * 2 + (3 * KT + m)], spill[:, m, :]).then_inc(S(f"spilled{m}"), 16)
                for b in range(2):
                    evicted(act, units("dt") + b)
                A(dtmp[:, :, :], dt[:, :, :], ACT.Abs).then_inc(S("dt_act"), 1)
                load_functions(EXP_AND_LN)
                act.wait_ge(S("dt_act"), 1)
                A(dtmp[:, :, :], dtmp[:, :, :], ACT.Exp, scale=-1.0).then_inc(S("dt_act"), 1)
                act.wait_ge(S("dt_act"), 2)
                A(dtmp[:, :, :], dtmp[:, :, :], ACT.Ln, bias=1.0).then_inc(S("dt_act"), 1)
                A(expA[:, :], col("A_log_3", 0, 16), ACT.Exp).then_inc(S("dt_act"), 1)
                act.wait_ge(S("dec_sum"), 1)
                A(dec[:, :, :, :].rearrange("p r c h -> p (r c h)"), banks[2][:, 0:3 * P], ACT.Exp
                  ).then_inc(S("dec_ready"), 1)

            def ssd(c, b):
                tok = bass.ds(c.value() * P, P) if c.i is not None else slice(c.b * P, (c.b + 1) * P)
                first = c.i is None and c.b == 0
                act.wait_ge(S("x_turned"), c.value(1))
                for q in range(2):
                    mm = A(xt[:, q * 512:(q + 1) * 512], banks[4 + q][:, :], ACT.Copy)
                mm.then_inc(S("xt_ready"), 1)
                act.wait_ge(S("b_turned"), c.value(1))
                A(bt[:, :], banks[6][:, :], ACT.Copy).then_inc(S("bt_ready"), 1)
                for q in range(4):
                    act.wait_ge(S("seg_done"), (c.i * 8 if c.i is not None else 0) + (c.b * 4 + q + 1))
                    mm = A(lt[:, 4 * q:4 * q + 4, :], banks[seg_banks[q]][:, :].rearrange("p (h t) -> p h t", t=P),
                           ACT.Exp)
                mm.then_inc(S("lt_ready"), 1)
                act.wait_ge(S("gz_ready"), c.value(1))
                act.wait_ge(S("new_done"), c.value(1))
                A(xe[:, :], xd[:, :], ACT.Square).then_inc(S("ssd_square"), 1)
                act.wait_ge(S("ssd_sum"), c.value(1))
                A(rs[:, :, :], banks[6][:, :].rearrange("p (g t) -> p g t", t=P), ACT.Sqrt, bias=eps[:, 0:1],
                  scale=SSD_GROUPS / D).then_inc(S("rs_ready"), 1)
                act.wait_ge(S("gn_ready"), c.value(1))
                settled(act)
                A(xh[:, :, tok], xd[:, :].rearrange("p (k t) -> p k t", t=P), ACT.Copy).then_inc(S("ssd_high"), 1)

            def load_chunk(c, b):
                tok = bass.ds(c.value() * P, P) if c.i is not None else slice(c.b * P, (c.b + 1) * P)
                act.dma_start(f[:, b], spills[3 * KT:3 * KT + 16, :, tok].rearrange("k p t -> p k t")
                              ).then_inc(S(f"f_in{b}"), 16)
                act.dma_start(zf[:, b], spills[2 * KT:3 * KT, :, tok].rearrange("k p t -> p k t")
                              ).then_inc(S(f"f_in{b}"), 16)

            if "ssd_out" in run:
                for m in range(2):
                    act.wait_ge(S(f"spilled{m}"), 16 * (12 + KT))
                for i in turns(act, CHUNKS // 2):
                    for b in range(2):
                        if not isinstance(i, int):
                            act.wait_ge(S("ssd_low"), i * 2)
                        load_chunk(at(i, 2, b), b)
                    for b in range(2):
                        ssd(at(i, 2, b), b)

            def s5_pair_inputs(n):
                act.dma_start(bc[:, :, :, :], ins["s5_bc"][n]).then_inc(S("bc_in"), 16)

            def s5_inputs(n):
                if not isinstance(n, int):
                    act.wait_ge(S("pb_ready"), n)
                s5_pair_inputs(n)
                act.wait_ge(S("w1_turned"), n + 1)
                if not isinstance(n, int):
                    act.wait_ge(S("s5_in"), n)
                settled(act)
                for c in range(2):
                    for par in range(2):
                        states = slice(par * S5_N, (par + 1) * S5_N)
                        mm = A(wz[:, par, c, :, states],
                               banks[2 + c][:, :].rearrange("p (q n) -> p q n", n=P)[:, :, states], ACT.Copy)
                mm.then_inc(S("w1_ready"), 1)
                act.wait_ge(S("gm_done"), n + 1)
                if not isinstance(n, int):
                    act.wait_ge(S("w3_in"), n * 128)
                for par in range(2):
                    mm = A(gm.rearrange("p (q a) h -> p a q h", a=2)[:, par],
                           banks[6 + par][:, 0:4 * S5_H].rearrange("p (q h) -> p q h", h=S5_H), ACT.Copy)
                mm.then_inc(S("gm_ready"), 1)
                act.wait_ge(S("gm_ready"), n + 1)
                for tau in range(S5_TAU):
                    rows = (tau + 1) * S5_H
                    act.dma_start(w3[0:rows, :, tau, :], gm[P - rows:P]).then_inc(S("w3_in"), 16)
                act.wait_ge(S("s5_in"), n + 1)
                settled(act)
                for c in range(2):
                    at_ = bass.ds(n * 4, 4) if not isinstance(n, int) else slice(0, 4)
                    mm = A(s5[:, c, at_, :], banks[4 + c][:, :].rearrange("p (q b) -> p q b", b=P), ACT.Copy)
                mm.then_inc(S("s5_stored"), 1)

            def s5_outputs(n):
                if not isinstance(n, int):
                    act.wait_ge(S("pc_ready"), n)
                s5_pair_inputs(n)
                act.wait_ge(S("pc_ready"), n + 1)
                if not isinstance(n, int):
                    act.wait_ge(S("s5_carried"), n)
                settled(act)
                for par in range(2):
                    rows = slice(par * S5_N, (par + 1) * S5_N)
                    mm = A(wz[rows, par], pb[rows].rearrange("p c q a h -> p c q (a h)"), ACT.Copy)
                mm.then_inc(S("wc_ready"), 1)
                act.wait_ge(S("s5_added"), n + 1)
                at_ = bass.ds(n * 8, 8) if not isinstance(n, int) else slice(0, 8)
                for tau in range(S5_TAU):
                    act.dma_start(y_channels[:, at_, tau, :], u5[tau * S5_H:(tau + 1) * S5_H, at_, :]
                                  ).then_inc(S("y_stored"), 16)

            y_channels = y_spill.rearrange("(g h) t b -> h g t b", h=S5_H)
            if "glu" in run:
                all_evicted(act, "ssd_out")
                u_channels = spills[0:KT].rearrange("k p x -> (k p) x").rearrange(
                    "(g h) (t b) -> h g t b", h=S5_H, t=S5_TAU)
                for tau in range(S5_TAU):
                    act.dma_start(u5[tau * S5_H:(tau + 1) * S5_H, :, :], u_channels[:, :, tau, :]
                                  ).then_inc(S("u5_in"), 16)
                act.wait_ge(S("s5_small_in"), 16)
                A(s5c[:, 3, :], s5c[:, 2, :], ACT.Exp).then_inc(S("s5_act"), 1)
                act.wait_ge(S("s5_angles"), 1)
                A(s5c[:, 5, :], s5c[:, 4, :], ACT.Exp).then_inc(S("s5_act"), 1)
                A(s5c[:, 7, :], s5c[:, 6, :], ACT.Sin).then_inc(S("s5_act"), 1)
                A(s5c[:, 8, :], s5c[:, 6, :], ACT.Sin, scale=0.5).then_inc(S("s5_act"), 1)
                act.wait_ge(S("w3_zero"), 1)
                for i in turns(act, KT):
                    s5_inputs(i)
                act.wait_ge(S("wz_zero"), 1)
                for i in turns(act, KT):
                    s5_outputs(i)
                act.wait_ge(S("y_stored"), KT * S5_TAU * 16)
                act.dma_start(y5[:, :, :].rearrange("p k (t b) -> p k t b", t=S5_TAU),
                              y_spill.rearrange("(k p) t b -> p k t b", p=P)).then_inc(S("y5_in"), 16)
                act.wait_ge(S("y5_in"), 16)
                for k in range(KT):
                    if k >= 2:
                        act.wait_ge(S("yg_low"), k - 1)
                    A(yg[:, k % 2, :].rearrange("p (b t) -> p b t", t=S5_TAU),
                      y5[:, k, :].rearrange("p (t b) -> p b t", t=S5_TAU), ACT.Gelu_apprx_tanh
                      ).then_inc(S("yg_ready"), 1)
                    act.wait_ge(S("yg_ready"), k + 1)
                    A(xh[:, k, :], yg[:, k % 2, :], ACT.Copy).then_inc(S("yg_high"), 1)
                for i in range(4):
                    unit = units("glu") + i * UNITS["glu"]
                    if i:
                        act.wait_ge(S("v_ready"), 4 * i)
                    act.dma_start(z5[:, :, :], spills[KT + 2 * i:KT + 2 * i + 2].rearrange("k p t -> p k t")
                                  ).then_inc(S("z5_in"), 16)
                    for m in range(2):
                        for th in range(2):
                            e = 4 * i + 2 * m + th
                            produced(act, unit + (2 * m + th))
                            if e >= 2:
                                act.wait_ge(S("v_ready"), e - 1)
                            A(sig5[:, th, :], banks[th][:, :], ACT.Sigmoid, bias=col("s5_b_glu_3", 2 * i + m)
                              ).then_inc(S(f"bank_free{th}"), 1)
                        for th in range(2):
                            e = 4 * i + 2 * m + th
                            act.wait_ge(S("v_ready"), e + 1)
                            A(vh[:, m, th * HALF:(th + 1) * HALF], vt5[:, th, :], ACT.Copy
                              ).then_inc(S("vh_ready"), 1)
                all_evicted(act, "glu")
                side_take("side3", ins["p3"], 2)
            if "gate3" in run:
                all_evicted(act, "side3")
                norm(8, 6)
                gate_take("gate3", 1)
                act.wait_ge(S("h_added"), 32)
                norm(9, None, "keep")
            act.wait_ge(S("h_final"), 1)
            for k in range(KT):
                act.dma_start(out[:, k, :], h[:, k, :]).then_inc(S("stored"), 16)

        @block.vector
        def _(dve):
            V = nc.vector

            def norm(n, sn, gain, mode="split", src=h):
                acc, hn, rinv = nb["acc"], nb["hn"], nb["rinv"]
                for k in range(KT):
                    dve.wait_ge(S("norm_square"), n * KT + k + 1)
                    if k == 0:
                        V.tensor_copy(acc[:, :], nb["sq"][:, 0, :]).then_inc(S("norm_acc"), 1)
                    else:
                        dve.wait_ge(S("norm_acc"), n * KT + k)
                        V.tensor_tensor(acc[:, :], acc[:, :], nb["sq"][:, k % 2, :], ALU.add
                                        ).then_inc(S("norm_acc"), 1)
                for th in range(2):
                    t = slice(th * HALF, (th + 1) * HALF)
                    dve.wait_ge(S("norm_root"), 2 * n + th + 1)
                    V.reciprocal(rinv[:, t], rinv[:, t]).then_inc(S("norm_rinv"), 1)
                dve.wait_ge(S("norm_rinv"), 2 * n + 2)

                def scale(k):
                    g = gain(k)
                    if mode == "keep":
                        V.scalar_tensor_tensor(h[:, k, :], h[:, k, :], g, rinv[:, :], ALU.mult, ALU.mult
                                               ).then_inc(S("norm_scaled"), 1)
                        return
                    if k >= 2:
                        dve.wait_ge(S("norm_low"), sn * KT + k - 1)
                    V.scalar_tensor_tensor(hn[:, k % 2, :], src[:, k, :], g, rinv[:, :], ALU.mult, ALU.mult
                                           ).then_inc(S("norm_scaled"), 1)

                def low(k):
                    dve.wait_ge(S("norm_high"), sn * KT + k + 1)
                    if mode == "mod":
                        V.scalar_tensor_tensor(xl[:, k, :], hn[:, k % 2, :], mod[:, k:k + 1],
                                               xh[:, k, :].bitcast(F32), ALU.add, ALU.subtract
                                               ).then_inc(S("norm_low"), 1)
                    else:
                        V.tensor_tensor(xl[:, k, :], hn[:, k % 2, :], xh[:, k, :].bitcast(F32), ALU.subtract
                                        ).then_inc(S("norm_low"), 1)

                for k in range(KT):
                    scale(k)
                    if k and mode != "keep":
                        low(k - 1)
                if mode != "keep":
                    low(KT - 1)

            def gain(name):
                return lambda k: col(name, k)

            def add_tiles(unit, gates=None):
                for n in range(KT):
                    for th in range(2):
                        t = slice(th * HALF, (th + 1) * HALF)
                        produced(dve, unit + (2 * n + th))
                        if gates is None:
                            V.tensor_tensor(h[:, n, t], banks[th][:, :], h[:, n, t], ALU.add
                                            ).then_inc(S(f"bank_free{th}"), 1)
                        else:
                            V.scalar_tensor_tensor(h[:, n, t], banks[th][:, :], gates(n), h[:, n, t],
                                                   ALU.mult, ALU.add).then_inc(S(f"bank_free{th}"), 1)

            dve.wait_ge(S("setup"), 64)
            norm(0, 0, gain("norm_mix"))
            dve.wait_ge(S("ch_ready"), 1)
            V.tensor_tensor(cl[:, :, :], cf[:, :, :], ch[:, :, :].bitcast(F32), ALU.subtract
                            ).then_inc(S("cl_ready"), 1)
            with dve.Fori(0, PAIRS) as j:
                unit = units("attn", j)
                for th in range(2):
                    produced(dve, unit + (2 + th))
                    V.tensor_copy(kT[:, th * HALF:(th + 1) * HALF], banks[th][:, :]
                                  ).then_inc(S(f"bank_free{th}"), 1)

                def soft(s):
                    c0, z = first_col[s], banks[4 + s % 2]
                    dve.wait_ge(S("log_ready"), j * NS + (s + 1))
                    if s >= 4:
                        dve.wait_ge(S("cum_done"), j * n_cum + cum2[s - 4])
                    V.scalar_tensor_tensor(spb[:, s % 4, c0:], z[:, c0:], 0.0, lb[:, s % 2, c0:], ALU.max, ALU.add
                                           ).then_inc(S("sp_ready"), 1)
                    if s >= 4:
                        dve.wait_ge(S("a_ready"), j * NS + (s - 3))
                    V.scalar_tensor_tensor(wb[:, s % 4, c0:], z[:, c0:], 0.0, lb[:, s % 2, c0:], ALU.min,
                                           ALU.subtract).then_inc(S("w_ready"), 1)

                def exponent(s):
                    c0 = first_col[s]
                    dve.wait_ge(S("w_ready"), j * NS + (s + 1))
                    dve.wait_ge(S("cum_done"), j * n_cum + cum1[s])
                    V.tensor_tensor(wb[:, s % 4, c0:], wb[:, s % 4, c0:], banks[6 + steps[s][2]][:, c0:],
                                    ALU.subtract).then_inc(S("e_ready"), 1)

                for s in range(NS + 1):
                    if s < NS:
                        soft(s)
                    if s >= 1:
                        exponent(s - 1)
                for th in range(2):
                    t = slice(th * HALF, (th + 1) * HALF)
                    dve.wait_ge(S("oh_ready"), j * 2 + (th + 1))
                    V.tensor_tensor(ol[:, t], banks[2 + th][:, :], oh[:, t].bitcast(F32), ALU.subtract
                                    ).then_inc(S("ol_ready"), 1)
                add_tiles(unit + 6)

            if "ffn_first" in run:
                norm(1, 1, gain("norm_ffn"))

                def hidden(unit, gh_before, parity):
                    for m in range(2):
                        for th in range(2):
                            evicted(dve, unit + (4 * m + th))
                            produced(dve, unit + (4 * m + 2 + th))
                            if m or unit.i is not None:
                                dve.wait_ge(S("gl_ready"), gh_before + (2 * m + th - 1))
                            V.tensor_tensor(gt[:, th, :], sa[:, th, :], banks[th][:, :], ALU.mult
                                            ).then_inc(S(f"bank_free{th}"), 1)
                        for th in range(2):
                            dve.wait_ge(S("gh_ready"), gh_before + (2 * m + th + 1))
                            V.tensor_tensor(gl[:, parity, m, th * HALF:(th + 1) * HALF], gt[:, th, :],
                                            gh[:, parity, m, th * HALF:(th + 1) * HALF].bitcast(F32),
                                            ALU.subtract).then_inc(S("gl_ready"), 1)

                def modulation(unit, tile):
                    produced(dve, unit)
                    c = COLS["ada_b_2"][0]
                    if isinstance(tile, int):
                        m_, b_ = mod[:, tile:tile + 1], cols[:, c + tile:c + tile + 1]
                    else:
                        m_, b_ = mod[:, bass.ds(tile, 1)], cols[:, bass.ds(tile + c, 1)]
                    V.tensor_tensor(m_, banks[unit.b % 2][:, 0:1], b_, ALU.add
                                    ).then_inc(S(f"bank_free{unit.b % 2}"), 1)

                hidden(units("ffn_first"), 0, 0)
                for m in range(4):
                    modulation(units("ffn_first") + (8 + m), m)
                with dve.Fori(0, TURNS["ffn"]) as i:
                    unit = units("ffn", i)
                    hidden(unit, i * 8 + 4, 1)
                    add_tiles(unit + 8)
                    hidden(unit + 24, i * 8 + 8, 0)
                    add_tiles(unit + 32)
                    for m in range(4):
                        modulation(unit + (48 + m), i * 4 + (4 + m))
                add_tiles(units("ffn_last"))

            def side_low(n):
                dve.wait_ge(S("ph_ready"), n)
                V.tensor_tensor(pl[:, :, :], pf[:, :, :], ph[:, :, :].bitcast(F32), ALU.subtract
                                ).then_inc(S("pl_ready"), 1)

            def gate_add(name, g):
                for m in range(2 * KT):
                    t = slice(m % 2 * HALF, (m % 2 + 1) * HALF)
                    evicted(dve, units(name) + m)
                    V.tensor_tensor(sg[:, m % 2, :], sg[:, m % 2, :], side[:, m // 2, t], ALU.mult
                                    ).then_inc(S("gated"), 1)
                    dve.wait_ge(S("gated"), 16 * g + m + 1)
                    V.tensor_tensor(h[:, m // 2, t], h[:, m // 2, t], sg[:, m % 2, :], ALU.add
                                    ).then_inc(S("h_added"), 1)

            if "side1" in run:
                side_low(1)
            if "gate1" in run:
                norm(2, 2, gain("norm_ple"))
                gate_add("gate1", 0)
                norm(3, None, gain("final_norm"), "keep")
            if "conv" in run:
                V.scalar_tensor_tensor(modg[:, :], mod[:, 8:16], 1.0, col("norm_g_2", 0, 8), ALU.add, ALU.mult
                                       ).then_inc(S("modg_ready"), 1)
                dve.wait_ge(S("modg_ready"), 1)
                dve.wait_ge(S("norm_scaled"), 4 * KT)
                norm(4, 3, lambda k: modg[:, k:k + 1], "mod")
                dve.wait_ge(S("norm_low"), 4 * KT)
                V.memset(apad[:, 0:CONV_TAPS - 1], 0.0).then_inc(S("apad_zero"), 1)
                dve.wait_ge(S("apad_zero"), 1)

            def convolution(i):
                unit, n = units("conv", i), 0 if i is None else i
                for th in range(2):
                    evicted(dve, unit + th)
                    produced(dve, unit + (2 + th))
                    if i is not None:
                        dve.wait_ge(S("conv_done"), n)
                    o = CONV_TAPS - 1 + th * HALF
                    V.tensor_tensor(apad[:, o:o + HALF], sigb[:, th * HALF:(th + 1) * HALF], banks[th][:, :],
                                    ALU.mult).then_inc(S(f"bank_free{th}"), 1)
                evicted(dve, unit + 3)
                w0 = COLS["conv_w_2"][0]

                def w(k):
                    if i is None:
                        return cols[:, w0 + k:w0 + k + 1]
                    return cols[:, bass.ds(n * CONV_TAPS + (w0 + k), 1)]

                bias = col("conv_b_2", 0) if i is None else cols[:, bass.ds(n + COLS["conv_b_2"][0], 1)]
                for k in range(CONV_TAPS):
                    acc, a_in = cacc[:, k % 2, :], apad[:, k:k + T]
                    if k >= 2:
                        dve.wait_ge(S("conv_step"), n * CONV_TAPS + (k - 1))
                    if k == 0:
                        mm = V.tensor_scalar(acc, a_in, w(k), bias, ALU.mult, ALU.add)
                    elif k == 1:
                        mm = V.tensor_scalar(acc, a_in, w(k), None, ALU.mult)
                    else:
                        mm = V.scalar_tensor_tensor(acc, a_in, w(k), acc, ALU.mult, ALU.add)
                    mm.then_inc(S("conv_step"), 1)
                dve.wait_ge(S("conv_step"), n * CONV_TAPS + CONV_TAPS)
                if i is not None:
                    dve.wait_ge(S("conv_stored"), n * 16)
                V.tensor_tensor(cout[:, :], cacc[:, 0, :], cacc[:, 1, :], ALU.add).then_inc(S("conv_done"), 1)

            if "conv" in run:
                convolution(None)
                with dve.Fori(1, KT) as i:
                    convolution(i)

            def retention(i):
                unit, n = units("ret", i), 0 if i is None else i
                dve.wait_ge(S("tabs_in"), n * 16 + 16)
                for x, dst in enumerate((qr, kr)):
                    u0 = unit + 4 * x
                    cos, sin = tabs[:, 2 * x, :], tabs[:, 2 * x + 1, :]
                    for th in range(2):
                        t = slice(th * HALF, (th + 1) * HALF)
                        produced(dve, u0 + th)
                        V.tensor_tensor(dst[:, 0, t], cos[:, t], banks[th][:, :], ALU.mult)
                        V.tensor_tensor(dst[:, 1, t], sin[:, t], banks[th][:, :], ALU.mult
                                        ).then_inc(S(f"bank_free{th}"), 1)
                    for th in range(2):
                        t = slice(th * HALF, (th + 1) * HALF)
                        produced(dve, u0 + (2 + th))
                        if th or x:
                            dve.wait_ge(S("rope_done"), n * 8 + (4 * x + 2 * th))
                        elif i is not None:
                            dve.wait_ge(S("ry_done"), n * 2)
                        V.tensor_tensor(rt[:, 0, :], sin[:, t], banks[th][:, :], ALU.mult)
                        V.tensor_tensor(rt[:, 1, :], cos[:, t], banks[th][:, :], ALU.mult
                                        ).then_inc(S(f"bank_free{th}"), 1)
                        evicted(dve, u0 + (2 + th))
                        V.tensor_tensor(dst[:, 0, t], dst[:, 0, t], rt[:, 0, :], ALU.subtract
                                        ).then_inc(S("rope_done"), 1)
                        V.tensor_tensor(dst[:, 1, t], dst[:, 1, t], rt[:, 1, :], ALU.add
                                        ).then_inc(S("rope_done"), 1)
                for s, c0 in enumerate(ret_col):
                    if ret_diag_no[s]:
                        dve.wait_ge(S("ret_scores"), n * RS + (s + 1))
                        if s >= 2:
                            dve.wait_ge(S("ret_values"), n * RS + (s - 1))
                        V.tensor_tensor(pt[:, s % 2, c0:c0 + P], banks[4 + s % 2][:, c0:c0 + P], M["upto"], ALU.mult
                                        ).then_inc(S("p_diag"), 1)
                dve.wait_ge(S("o_ready"), n * 4 + 4)
                for th in range(2):
                    dve.wait_ge(S("ret_sum"), n * 4 + (th + 1))
                    for m in range(2):
                        o = ot[:, m, th * HALF:(th + 1) * HALF]
                        V.scalar_tensor_tensor(o, banks[2 + th][:, :], -1.0 / RET_DIM, o, ALU.mult, ALU.add
                                               ).then_inc(S("o_centered"), 1)
                for th in range(2):
                    dve.wait_ge(S("r_root"), n * 2 + (th + 1))
                    V.reciprocal(rt[:, th, :], rt[:, th, :]).then_inc(S("r_inv"), 1)
                dve.wait_ge(S("r_inv"), n * 2 + 2)
                dve.wait_ge(S("rg_in"), n * 16 + 16)

                def c(name, m):
                    c0 = COLS[name][0] + m
                    return cols[:, c0:c0 + 1] if i is None else cols[:, bass.ds(n * 2 + c0, 1)]

                for m in range(2):
                    V.scalar_tensor_tensor(ot[:, m, :], ot[:, m, :], c("ret_gn_g_2", m),
                                           rt[:, :, :].rearrange("p a t -> p (a t)"), ALU.mult, ALU.mult
                                           ).then_inc(S("r_scaled"), 1)
                    dve.wait_ge(S("r_scaled"), n * 2 + (m + 1))
                    V.scalar_tensor_tensor(ot[:, m, :], ot[:, m, :], c("ret_gn_b_2", m), rg[:, m, :], ALU.add,
                                           ALU.mult).then_inc(S("ry_done"), 1)
                for m in range(2):
                    dve.wait_ge(S("rh_ready"), n * 2 + (m + 1))
                    mm = V.tensor_tensor(rl[:, m, :], ot[:, m, :], rh[:, m, :].bitcast(F32), ALU.subtract)
                mm.then_inc(S("rl_ready"), 1)
                add_tiles(unit + 12, lambda n: mod[:, 16 + n:17 + n])

            if "ret" in run:
                retention(None)
                with dve.Fori(1, RET_HEADS) as i:
                    retention(i)

            if "pw" in run:
                dve.wait_ge(S("cv_in"), 16)
                V.tensor_tensor(nb["acc"][:, :], cv[:, 0, :], cv[:, 1, :], ALU.add).then_inc(S("mean_acc"), 2)
                for k in range(2, KT):
                    dve.wait_ge(S("mean_acc"), k)
                    V.tensor_tensor(nb["acc"][:, :], nb["acc"][:, :], cv[:, k, :], ALU.add
                                    ).then_inc(S("mean_acc"), 1)
                for th in range(2):
                    dve.wait_ge(S("mean_sum"), th + 1)
                    for k in range(KT):
                        c_ = cv[:, k, th * HALF:(th + 1) * HALF]
                        V.scalar_tensor_tensor(c_, banks[2 + th][:, :], -1.0 / D, c_, ALU.mult, ALU.add
                                               ).then_inc(S("ln_centered"), 1)
                dve.wait_ge(S("ln_centered"), 2 * KT)
                norm(5, 4, gain("conv_ln_g_2"), "silu", cv)
                with dve.Fori(0, 4) as i:
                    unit = units("pw", i)
                    dve.wait_ge(S("cg_in"), i * 16 + 16)
                    for m in range(2):
                        for th in range(2):
                            t = slice(th * HALF, (th + 1) * HALF)
                            produced(dve, unit + (2 * m + th))
                            if m:
                                dve.wait_ge(S("yl_ready"), i * 4 + (th + 1))
                            V.tensor_tensor(yt[:, th, :], cg[:, m, t], banks[th][:, :], ALU.mult
                                            ).then_inc(S(f"bank_free{th}"), 1)
                        for th in range(2):
                            t = slice(th * HALF, (th + 1) * HALF)
                            dve.wait_ge(S("yh_ready"), i * 4 + (2 * m + th + 1))
                            V.tensor_tensor(yl[:, m, t], yt[:, th, :], yh[:, m, t].bitcast(F32), ALU.subtract
                                            ).then_inc(S("yl_ready"), 1)
                    add_tiles(unit + 4, lambda n: mod[:, 16 + n:17 + n])
                norm(6, None, gain("final_g_2"), "keep")

            if "s5_u" in run:
                dve.wait_ge(S("norm_scaled"), 7 * KT)
                norm(7, 5, gain("norm_w_3"))
                dve.wait_ge(S("norm_low"), 6 * KT)
                V.memset(xc[:, :, 0:SSD_TAPS - 1], 0.0).then_inc(S("xc_zero"), 1)
                dve.wait_ge(S("xc_zero"), 1)
                for i in turns(dve, KT):
                    n, unit = i, units("xbc", None if isinstance(i, int) else i)
                    for m in range(2):
                        evicted(dve, unit + (2 * m + 1))
                        evicted(dve, unit + 2 * m)
                        dve.wait_ge(S(f"spilled{m}"), (n + 12) * 16)
                        cw = COLS["conv_w_3"][0]
                        for k in range(SSD_TAPS):
                            if isinstance(n, int):
                                w = cols[:, cw + m * SSD_TAPS + k:cw + m * SSD_TAPS + k + 1]
                                bias = col("conv_b_3", m)
                            else:
                                w = cols[:, bass.ds(n * (2 * SSD_TAPS) + (cw + m * SSD_TAPS + k), 1)]
                                bias = cols[:, bass.ds(n * 2 + (COLS["conv_b_3"][0] + m), 1)]
                            o, a_in = spill[:, m, :], xc[:, m, k:k + T]
                            if k == 0:
                                V.tensor_scalar(o, a_in, w, bias, ALU.mult, ALU.add).then_inc(S("x_step"), 1)
                                continue
                            dve.wait_ge(S("x_step"), n * 6 + (3 * m + k))
                            V.scalar_tensor_tensor(o, a_in, w, o, ALU.mult, ALU.add).then_inc(
                                S("x_step" if k < SSD_TAPS - 1 else "xo_ready"), 1)
                for b in range(2):
                    produced(dve, units("dt") + b)
                    V.tensor_tensor(dt[:, 4 * b:4 * b + 4, :],
                                    banks[b][:, 0:64].rearrange("p (c h) -> p c h", h=SSD_HEADS),
                                    col("dt_bias_3", 0, 16).unsqueeze(1).broadcast_to([P, 4, SSD_HEADS]), ALU.add
                                    ).then_inc(S(f"bank_free{b}"), 1)
                dve.wait_ge(S("dt_act"), 4)
                V.scalar_tensor_tensor(dt[:, :, :], dt[:, :, :], 0.0, dtmp[:, :, :], ALU.max, ALU.add
                                       ).then_inc(S("dt_ready"), 1)
                dve.wait_ge(S("dt_ready"), 1)
                V.scalar_tensor_tensor(da[:, :, :], dt[:, :, :], -1.0,
                                       expA[:, :].unsqueeze(1).broadcast_to([P, CHUNKS, SSD_HEADS]), ALU.mult,
                                       ALU.mult).then_inc(S("da_ready"), 1)
                dve.wait_ge(S("da_ready"), 1)

            def ssd(c, b):
                n = c.value()
                first = c.i is None and c.b == 0

                def heads(t, q):
                    return t[:, q * 512:(q + 1) * 512].rearrange("p (h d) -> p h d", d=SSD_P)

                def per_head(t, q):
                    return t[:, 8 * q:8 * q + 8].unsqueeze(2).broadcast_to([P, 8, SSD_P])

                def chunk_of(t):
                    return t[:, n, :]

                if not first:
                    dve.wait_ge(S("ssd_low"), n)
                V.tensor_tensor(mt[:, :, :], M["upto"].unsqueeze(1).broadcast_to([P, SSD_HEADS, P]),
                                chunk_of(da).unsqueeze(2).broadcast_to([P, SSD_HEADS, P]), ALU.mult
                                ).then_inc(S("mt_ready"), 1)
                dve.wait_ge(S("xt_ready"), c.value(1))
                for q in range(2):
                    mm = V.tensor_tensor(heads(xd, q), heads(xt, q), per_head(chunk_of(dt), q), ALU.mult)
                mm.then_inc(S("xd_ready"), 1)
                dve.wait_ge(S("xd_ready"), c.value(1))
                dve.wait_ge(S("dec_ready"), 1)
                for q in range(2):
                    mm = V.tensor_tensor(heads(xe, q), heads(xd, q), per_head(dec[:, 1, n, :], q), ALU.mult)
                mm.then_inc(S("xe_ready"), 1)
                dve.wait_ge(S("bc_done"), c.value(1))
                V.tensor_tensor(sm[:, :, :], banks[4][:, :].rearrange("p (g t) -> p g t", t=P),
                                M["upto"].unsqueeze(1).broadcast_to([P, SSD_GROUPS, P]), ALU.mult
                                ).then_inc(S("sm_ready"), 1)
                dve.wait_ge(S("sm_ready"), c.value(1))
                dve.wait_ge(S("lt_ready"), c.value(1))
                l4 = lt[:, :, :].rearrange("p (g h) t -> p g h t", g=SSD_GROUPS)
                V.tensor_tensor(l4, l4, sm[:, :, :].unsqueeze(2).broadcast_to([P, SSD_GROUPS, 4, P]), ALU.mult
                                ).then_inc(S("w_masked"), 1)
                dve.wait_ge(S("inter_done"), c.value(1))
                for q in range(2):
                    mm = V.tensor_tensor(heads(ys, q), banks[4 + q][:, :].rearrange("p (h d) -> p h d", d=SSD_P),
                                         per_head(dec[:, 0, n, :], q), ALU.mult)
                mm.then_inc(S("ssd_y"), 1)
                for q in range(2):
                    mm = V.tensor_tensor(heads(yd, q), heads(xt, q), per_head(col("ssd_D_3", 0, 16), q), ALU.mult)
                mm.then_inc(S("ssd_yd"), 1)
                dve.wait_ge(S("ssd_y"), c.value(1))
                dve.wait_ge(S("intra_done"), c.value(1))
                for q in range(2):
                    y = ys[:, q * 512:(q + 1) * 512]
                    mm = V.tensor_tensor(y, y, banks[2 + q][:, :], ALU.add)
                mm.then_inc(S("ssd_yi"), 1)
                dve.wait_ge(S("ssd_yi"), c.value(1))
                V.tensor_tensor(ys[:, :], ys[:, :], yd[:, :], ALU.add).then_inc(S("ys_ready"), 1)
                for q in range(2):
                    mm = V.tensor_tensor(heads(state, q), heads(state, q), per_head(dec[:, 2, n, :], q), ALU.mult)
                mm.then_inc(S("state_decayed"), 1)
                dve.wait_ge(S("state_decayed"), c.value(1))
                dve.wait_ge(S("new_done"), c.value(1))
                for q in range(2):
                    y = state[:, q * 512:(q + 1) * 512]
                    mm = V.tensor_tensor(y, y, banks[6 + q][:, :], ALU.add)
                mm.then_inc(S("state_ready"), 1)
                dve.wait_ge(S("y_turned"), c.value(1))
                for q in range(2):
                    mm = V.tensor_tensor(xd[:, q * 512:(q + 1) * 512], zf[:, b, 4 * q:4 * q + 4, :].rearrange(
                        "p k t -> p (k t)"), banks[4 + q][:, :], ALU.mult)
                mm.then_inc(S("gz_ready"), 1)
                dve.wait_ge(S("ssd_square"), c.value(1))
                x8 = xd[:, :].rearrange("p (k t) -> p k t", t=P)
                V.tensor_tensor(x8, x8, col("ssd_norm_w_3", 0, 8).unsqueeze(2).broadcast_to([P, KT, P]), ALU.mult
                                ).then_inc(S("ssd_gain"), 1)
                dve.wait_ge(S("rs_ready"), c.value(1))
                V.reciprocal(rs[:, :, :], rs[:, :, :]).then_inc(S("rs_inv"), 1)
                dve.wait_ge(S("ssd_gain"), c.value(1))
                dve.wait_ge(S("rs_inv"), c.value(1))
                x4 = xd[:, :].rearrange("p (g m t) -> p g m t", g=SSD_GROUPS, t=P)
                V.tensor_tensor(x4, x4, rs[:, :, :].unsqueeze(2).broadcast_to([P, SSD_GROUPS, 2, P]), ALU.mult
                                ).then_inc(S("gn_ready"), 1)
                dve.wait_ge(S("ssd_high"), c.value(1))
                tok = bass.ds(n * P, P) if c.i is not None else slice(n * P, (n + 1) * P)
                V.tensor_tensor(xl[:, :, tok], x8, xh[:, :, tok].bitcast(F32), ALU.subtract
                                ).then_inc(S("ssd_low"), 1)

            if "ssd_out" in run:
                all_evicted(dve, "dt")
                V.memset(state[:, :], 0.0).then_inc(S("state_ready"), 1)
                dve.wait_ge(S("state_ready"), 1)
                for i in turns(dve, CHUNKS // 2):
                    for b in range(2):
                        ssd(at(i, 2, b), b)
                add_tiles(units("ssd_out"))

            class Chain:

                def __init__(self, sem, base=0, turn=0, per_turn=0):
                    self.sem, self.n = sem, 0
                    self.at = lambda n: base + n if isinstance(turn, int) else turn * per_turn + (base + n)

                def __call__(self, ins):
                    self.n += 1
                    ins.then_inc(S(self.sem), 1)
                    dve.wait_ge(S(self.sem), self.at(self.n))

            TT = V.tensor_tensor

            def complex_product(link, out, x, y, tmp, conj=False):
                link(TT(tmp[0], x[0], y[0], ALU.mult))
                link(TT(tmp[1], x[1], y[1], ALU.mult))
                link(TT(out[0], tmp[0], tmp[1], ALU.subtract))
                link(TT(tmp[0], x[0], y[1], ALU.mult))
                link(TT(tmp[1], x[1], y[0], ALU.mult))
                if conj:
                    link(V.scalar_tensor_tensor(out[1], tmp[0], -1.0, tmp[1], ALU.mult, ALU.subtract))
                else:
                    link(TT(out[1], tmp[0], tmp[1], ALU.add))

            def s5_coefficients():
                link = Chain("s5_small")
                k = [s5c[:, j, :] for j in range(12)]
                dve.wait_ge(S("s5_act"), 1)
                link(TT(k[4], k[0], k[3], ALU.mult))
                link(TT(k[6], k[1], k[3], ALU.mult))
                link(V.tensor_scalar(k[9], k[6], 1.0 / TURN, ROUND, ALU.mult, ALU.add))
                link(V.tensor_scalar(k[9], k[9], ROUND, None, ALU.subtract))
                for part in TURN_PARTS:
                    link(V.scalar_tensor_tensor(k[6], k[9], -part, k[6], ALU.mult, ALU.add))
                link(V.tensor_scalar(k[6], k[6], float(np.float32(np.pi)), -float(np.float32(np.pi)),
                                     ALU.min, ALU.max))
                V.tensor_copy(k[10], k[6]).then_inc(S("s5_angles"), 1)
                dve.wait_ge(S("s5_act"), 4)
                link(TT(k[8], k[8], k[8], ALU.mult))
                link(V.tensor_scalar(k[8], k[8], -2.0, 1.0, ALU.mult, ALU.add))
                pr, pi = s5p[:, 0], s5p[:, 1]
                link(V.memset(pr[:, 0, :], 1.0))
                link(V.memset(pi[:, 0, :], 0.0))
                link(TT(pr[:, 1, :], k[5], k[8], ALU.mult))
                link(TT(pi[:, 1, :], k[5], k[7], ALU.mult))
                for j in range(2, S5_TAU + 1):
                    complex_product(link, (pr[:, j, :], pi[:, j, :]), (pr[:, j - 1, :], pi[:, j - 1, :]),
                                    (pr[:, 1, :], pi[:, 1, :]), (k[9], k[10]))
                for j in range(S5_TAU):
                    link(V.tensor_copy(s5r[:, :, S5_TAU - 1 - j, :], s5p[:, :, j, :]))
                link(TT(k[9], k[0], k[0], ALU.mult))
                link(TT(k[10], k[1], k[1], ALU.mult))
                link(TT(k[9], k[9], k[10], ALU.add))
                link(V.reciprocal(k[11], k[9]))
                link(V.tensor_scalar(k[3], pr[:, 1, :], -1.0, None, ALU.add))
                link(TT(k[4], k[3], k[0], ALU.mult))
                link(TT(k[5], pi[:, 1, :], k[1], ALU.mult))
                link(TT(k[4], k[4], k[5], ALU.add))
                link(TT(k[5], pi[:, 1, :], k[0], ALU.mult))
                link(TT(k[6], k[3], k[1], ALU.mult))
                link(TT(k[5], k[5], k[6], ALU.subtract))
                link(TT(k[0], k[4], k[11], ALU.mult))
                link(TT(k[1], k[5], k[11], ALU.mult))

            def pairs_of(t, n):
                return t[:, bass.ds(n * 4, 4)] if not isinstance(n, int) else t[:, 4 * n:4 * n + 4]

            def powers(n, first):
                r = []
                for c in range(2):
                    q = s5p[:, c, first:first + S5_TAU, :] if first else s5r[:, c]
                    q = q[:, :, bass.ds(n * 4, 4)] if not isinstance(n, int) else q[:, :, 0:4]
                    r.append(q.rearrange("p a q -> p q a").unsqueeze(3).broadcast_to([P, 4, S5_TAU, S5_H]))
                return r

            tmp5 = [s5t[:, c] for c in range(2)]
            flat5 = [s5t[:, c].rearrange("p q a h -> p (q a h)") for c in range(2)]
            small5 = [t[:, 0:4 * S5_H].rearrange("p (q h) -> p q h", q=4) for t in flat5]

            def over_tau(t):
                return [t[:, c].unsqueeze(2).broadcast_to([P, 4, S5_TAU, S5_H]) for c in range(2)]

            def s5_inputs(n):
                dve.wait_ge(S("bc_in"), n * 16 + 16)
                if not isinstance(n, int):
                    dve.wait_ge(S("gm_done"), n)
                link = Chain("s5_chain", 0, n, 13)
                q = [pairs_of(s5c[:, c, :], n).unsqueeze(2).broadcast_to([P, 4, S5_H]) for c in range(2)]
                complex_product(link, (b0[:, 0], b0[:, 1]), q, (bc[:, 0], bc[:, 1]), (small5[0], small5[1]))
                link(V.tensor_copy(bm[:, 0], bc[:, 2]))
                b_, p_ = over_tau(b0), powers(n, 0)
                complex_product(link, (pb[:, 0], pb[:, 1]), b_, p_, tmp5)
                V.tensor_scalar(bm[:, 1], bc[:, 3], -1.0, None, ALU.mult).then_inc(S("pb_ready"), 1)
                dve.wait_ge(S("s5_local"), n + 1)
                for q in range(8):
                    d0 = COLS["s5_D_3"][0] + q
                    d_ = cols[:, d0:d0 + 1] if isinstance(n, int) else cols[:, bass.ds(n * 8 + d0, 1)]
                    mm = V.scalar_tensor_tensor(u5[:, u_at(n, q), :], u5[:, u_at(n, q), :], d_,
                                                banks[6 + q // 4][:, q % 4 * P:(q % 4 + 1) * P], ALU.mult, ALU.add)
                mm.then_inc(S("s5_local_added"), 1)

            def s5_outputs(n):
                dve.wait_ge(S("bc_in"), n * 16 + (KT + 1) * 16)
                if not isinstance(n, int):
                    dve.wait_ge(S("s5_carried"), n)
                link = Chain("s5_chain", 13 * KT, n, 6)
                c_ = [bc[:, 2 + c].unsqueeze(2).broadcast_to([P, 4, S5_TAU, S5_H]) for c in range(2)]
                complex_product(link, (pb[:, 0], pb[:, 1]), c_, powers(n, 1), tmp5, conj=True)
                V.tensor_copy(b0[:, 0], bc[:, 2]).then_inc(S("pc_ready"), 1)
                dve.wait_ge(S("s5_carried"), n + 1)
                for q in range(2):
                    g = bass.ds(n * 8 + 4 * q, 4) if not isinstance(n, int) else slice(4 * q, 4 * q + 4)
                    y = u5[:, g, 1:]
                    mm = TT(y, y, banks[4 + q][:, :].rearrange("p (g b) -> p g b", b=P)[:, :, 1:], ALU.add)
                mm.then_inc(S("s5_added"), 1)

            if "glu" in run:
                dve.wait_ge(S("s5_small_in"), 16)
                s5_coefficients()
                all_evicted(dve, "ssd_out")
                V.memset(wz[:, :, :, :, :], 0.0)
                V.memset(w3[:, :, :, :], 0.0).then_inc(S("w3_zero"), 1)
                dve.wait_ge(S("w3_zero"), 1)
                for i in turns(dve, KT):
                    s5_inputs(i)
                dve.wait_ge(S("s5_stored"), KT)
                link = Chain("s5_powers")
                link(V.tensor_copy(s5q[:, :, :, 0], s5p[:, :, S5_TAU, :]))
                m = 1
                while m < S5_RUN:
                    last_ = [s5q[:, c, :, m - 1:m].broadcast_to([P, S5_PAIRS, m]) for c in range(2)]
                    tmp = [t[:, 0:S5_PAIRS * m].rearrange("p (q j) -> p q j", j=m) for t in flat5]
                    complex_product(link, [s5q[:, c, :, m:2 * m] for c in range(2)],
                                    [s5q[:, c, :, 0:m] for c in range(2)], last_, tmp)
                    m *= 2
                runs = s5[:, :, :, :].rearrange("p c q (g j) -> p c q g j", j=S5_RUN)
                pb_flat = pb[:, :, :, :, :].rearrange("p c q a h -> p (c q a h)")
                s5t_flat = s5t[:, :, :, :, :].rearrange("p c q a h -> p (c q a h)")

                def advance(link, new, old, a, shape):
                    size = 2 * S5_PAIRS * shape[-1]
                    t1, t2 = [t[:, 0:size].rearrange("p (c q n) -> p c q n", c=2, q=S5_PAIRS)
                              for t in (pb_flat, s5t_flat)]
                    link(TT(t1, a[0], old, ALU.mult))
                    link(TT(t2, a[1], old, ALU.mult))
                    link(TT(new, new, t1, ALU.add))
                    link(TT(new[:, 0], new[:, 0], t2[:, 1], ALU.subtract))
                    link(TT(new[:, 1], new[:, 1], t2[:, 0], ALU.add))

                shape = [P, 2, S5_PAIRS, S5_RUNS]
                first_power = [s5q[:, c, :, 0:1].unsqueeze(1).broadcast_to(shape) for c in range(2)]
                with dve.Fori(1, S5_RUN) as j:
                    advance(Chain("s5_scan", -5, j, 5), runs[:, :, :, :, j], runs[:, :, :, :, j - 1],
                            first_power, shape)
                shape = [P, 2, S5_PAIRS, S5_RUN]
                every_power = [s5q[:, c].unsqueeze(1).broadcast_to(shape) for c in range(2)]
                link = Chain("s5_scan", 5 * (S5_RUN - 1))
                for g in range(1, S5_RUNS):
                    advance(link, runs[:, :, :, g, :],
                            runs[:, :, :, g - 1, S5_RUN - 1:S5_RUN].broadcast_to(shape), every_power, shape)
                V.memset(wz[:, :, :, :, :], 0.0).then_inc(S("wz_zero"), 1)
                for i in turns(dve, KT):
                    s5_outputs(i)
                for k in range(KT):
                    dve.wait_ge(S("yg_high"), k + 1)
                    TT(xl[:, k, :], yg[:, k % 2, :], xh[:, k, :].bitcast(F32), ALU.subtract
                       ).then_inc(S("yg_low"), 1)
                link = Chain("glu_step")
                for i in range(4):
                    unit = units("glu") + i * UNITS["glu"]
                    dve.wait_ge(S("z5_in"), 16 * (i + 1))
                    for m in range(2):
                        for th in range(2):
                            e, t = 4 * i + 2 * m + th, slice(th * HALF, (th + 1) * HALF)
                            v = vt5[:, th, :]
                            if e >= 2:
                                dve.wait_ge(S("vl_ready"), e - 1)
                            link(TT(v, xh[:, 2 * i + m, t].bitcast(F32), xl[:, 2 * i + m, t].bitcast(F32), ALU.add))
                            evicted(dve, unit + (2 * m + th))
                            link(TT(v, v, sig5[:, th, :], ALU.mult))
                            TT(v, v, z5[:, m, t], ALU.mult).then_inc(S("v_ready"), 1)
                        for th in range(2):
                            e, t = 4 * i + 2 * m + th, slice(th * HALF, (th + 1) * HALF)
                            dve.wait_ge(S("vh_ready"), e + 1)
                            TT(vl[:, m, t], vt5[:, th, :], vh[:, m, t].bitcast(F32), ALU.subtract
                               ).then_inc(S("vl_ready"), 1)
                    add_tiles(unit + 4)
                side_low(2)
            if "gate3" in run:
                norm(8, 6, gain("ple_norm_w_3"))
                gate_add("gate3", 1)
                norm(9, None, gain("final_norm_w_3"), "keep")
            dve.drain().then_inc(S("h_final"), 1)


def lay_out(a):
    def tiles(w):
        k, n = w.shape
        return w.reshape(k // P, P, n // P, P).transpose(2, 1, 0, 3)

    def slabs(w):
        k, n = w.shape
        return w.reshape(k // P, P, n // P, P).transpose(0, 2, 1, 3)

    def pack(parts):
        s = np.stack(parts)
        return s.reshape(-1, KT, P, P).transpose(0, 2, 1, 3)

    def out_pairs(w):
        s = slabs(w)
        return [pack([s[2 * c + t, n] for n in range(KT) for t in range(2)]) for c in range(s.shape[0] // 2)]

    stream = []
    qkv, wo = tiles(a["sb_w_in"][0]), slabs(a["sb_w_out"][0])
    for j in range(PAIRS):
        stream += [qkv[j], qkv[KT + j], qkv[2 * KT + j], pack(list(wo[j]))[0]]
    fin, fout = tiles(a["ffn_w_in"][0]), out_pairs(a["ffn_w_out"][0])
    nf, ada = D_FF // P, tiles(a["ada_w_2"][0])
    for c in range(FF_CHUNKS):
        for m in range(2):
            stream += [fin[2 * c + m], fin[nf + 2 * c + m]]
        if c:
            stream += list(fout[c - 1])
        if c % 2 == 0:
            stream += list(ada[2 * c:2 * c + 4])
    stream += list(fout[-1])
    stream += list(out_pairs(a["ple_w_proj"][0])[0])
    stream += list(tiles(a["ple_w_gate"][0]))
    w2, o2 = tiles(a["w_in_2"][0]), out_pairs(a["w_out_2"][0])
    for k in range(KT):
        stream += [w2[KT + k], w2[k], w2[2 * KT + k], w2[6 * KT + k]]
    for hd in range(RET_HEADS):
        for part in (3, 4, 5):
            stream += [w2[part * KT + 2 * hd], w2[part * KT + 2 * hd + 1]]
        stream += list(o2[4 + hd])
    pw = tiles(a["conv_pw_2"][0])
    for c in range(4):
        stream += [pw[2 * c], pw[2 * c + 1]] + list(o2[c])
    w3 = a["w_in_3"][0]
    stream += list(tiles(w3[:, :5 * D]))
    wdt = np.zeros((D, 2 * P), np.float32)
    wdt[:, :SSD_HEADS] = w3[:, 5 * D:]
    stream += list(tiles(wdt))
    stream += list(tiles(a["w_out_3"][0][D:]))
    glu, o3 = tiles(a["s5_w_glu_3"]  [0]), out_pairs(a["w_out_3"][0][:D])
    for c in range(4):
        stream += [glu[2 * c], glu[2 * c + 1]] + list(o3[c])
    stream += list(out_pairs(a["w_ple_proj_3"][0])[0])
    stream += list(tiles(a["w_ple_gate_3"][0]))
    stream = np.stack(stream).reshape(len(stream), P, KT * P)

    cols = np.zeros((P, N_COLS), np.float32)
    for name, (c, n) in COLS.items():
        w = np.asarray(a[name])
        if name in ("conv_w_2", "conv_w_3"):
            w = w[0].reshape(w.shape[1], n // w.shape[1], P).transpose(2, 1, 0)
            cols[:, c:c + n] = w.reshape(P, n)
        elif name == "s5_D_3":
            cols[:, c:c + n] = np.tile(w.reshape(S5_GROUPS, S5_H).T, (S5_TAU, 1))
        elif name in ("dt_bias_3", "A_log_3", "ssd_D_3"):
            cols[:, c:c + n] = np.broadcast_to(w.reshape(1, n), (P, n))
        else:
            cols[:, c:c + n] = w.reshape(n, P).T
    row, column = np.arange(P)[:, None], np.arange(P)[None, :]
    mats = np.stack([np.ones((P, P)), row == column, row > column, row <= column,
                     np.where(row >= column, MASKED, 0.0)], 1).astype(np.float32)

    def feature_major(x):
        return np.ascontiguousarray(x.T.reshape(-1, P, x.shape[0]).transpose(1, 0, 2))

    maps = {"wstream": stream, "cols": cols, "mats": mats, "x": feature_major(a["x"][0]),
            "p1": feature_major(a["p"][0, 0]), "p3": feature_major(a["p_3"][0, 0])}
    def pairs(x):
        x = x.reshape((S5_PAIRS, 2, S5_N) + x.shape[2:])
        return np.moveaxis(x, 0, 2).reshape((P, S5_PAIRS) + x.shape[3:])

    dt = np.broadcast_to(a["s5_log_dt_3"][0][:, None], (S5_GROUPS, S5_N))
    maps["s5_small"] = np.stack([pairs(a["s5_A_re_3"][0]), pairs(a["s5_A_im_3"][0]), pairs(dt)], 1)
    bc = np.stack([pairs(a["s5_B_re_3"][0]), pairs(a["s5_B_im_3"][0]),
                   pairs(a["s5_C_re_3"][0].transpose(0, 2, 1)), pairs(a["s5_C_im_3"][0].transpose(0, 2, 1))], 1)
    maps["s5_bc"] = bc.reshape(P, 4, KT, 4, S5_H).transpose(2, 0, 1, 3, 4)
    maps["rope"] = rope_tables()
    return maps




def rope_tables():
    half = RET_DIM // 2
    inv = (1.0 / (np.float32(10000.0) ** np.linspace(0.0, 1.0, half, dtype=np.float32))).astype(np.float32)
    theta = (np.arange(T, dtype=np.float32)[None, :] * inv[:, None]).astype(np.float64)
    out = np.zeros((RET_HEADS, P, 4, T), np.float32)
    for hd in range(RET_HEADS):
        g = 1.0 - 2.0 ** (-5.0 - hd)
        t = np.arange(T, dtype=np.float64)
        dq, dk = g ** t, g ** -t * RET_DIM ** -0.5
        for j, (f, d) in enumerate(((np.cos, dq), (np.sin, dq), (np.cos, dk), (np.sin, dk))):
            out[hd, :, j] = f(theta) * d
    return out


def kernel(**inputs):
    import concourse.bacc as bacc
    from concourse.bass_utils import run_bass_kernel_spmd as run

    nc = bacc.Bacc("TRN2", target_bir_lowering=False, num_devices=1, dynamic_dma_scratch_size=4096)
    arrays, args = {}, {}
    for name, a in lay_out({k: np.asarray(v) for k, v in inputs.items()}).items():
        a = np.ascontiguousarray(a)
        arrays[f"in_{name}"] = a
        args[name] = nc.dram_tensor(f"in_{name}", a.shape, mybir.dt.from_np(a.dtype), kind="ExternalInput").ap()
    out = nc.dram_tensor("out_y", (P, KT, T), F32, kind="ExternalOutput").ap()
    build(nc, args, out)
    r = run(nc, [arrays], core_ids=[0])
    y = r.results[0]["out_y"]
    return np.ascontiguousarray(y.transpose(2, 1, 0)).reshape(1, T, D)
```
